# Optimizing a Trainium2 kernel written in Bass

```python
import math
import jax, jax.numpy as jnp
from jax import lax
import numpy as np

D_MODEL = 1024
BATCH = 1
SEQ = 256
DEPTH = 1

D_MIX = D_MODEL
MOBA_HEADS = 8
MOBA_HEAD_DIM = 64
MOBA_WIDTH = MOBA_HEADS * MOBA_HEAD_DIM
MOBA_BLOCK = 256
MOBA_TOPK = 3
MOBA_QCHUNK = 128
ROPE_THETA = 500000.0
ROPE_DIM = MOBA_HEAD_DIM // 4
DN_HEADS = 4
DN_KEY_DIM = 128
DN_VAL_DIM = 128
DN_QK_WIDTH = DN_HEADS * DN_KEY_DIM
DN_WIDTH = DN_HEADS * DN_VAL_DIM
DN_CONV = 4
DN_CONV_CH = 2 * DN_QK_WIDTH + DN_WIDTH
DN_CHUNK = 64
IN_SPLITS = (MOBA_WIDTH, MOBA_WIDTH, MOBA_WIDTH, MOBA_WIDTH,
             DN_QK_WIDTH, DN_QK_WIDTH, DN_WIDTH, DN_WIDTH, DN_HEADS, DN_HEADS)
D_IN = sum(IN_SPLITS)
NORM_EPS = 1e-6
NEG_INF = -1e30

kernel_name = "hymba_moba_gated_deltanet_layer"

def rmsnorm(x, w):
    xf = x.astype(jnp.float32)
    y = xf * lax.rsqrt(jnp.mean(xf * xf, axis=-1, keepdims=True) + NORM_EPS)
    return (y * w.astype(jnp.float32)).astype(x.dtype)

def l2norm(x):
    return x * lax.rsqrt(jnp.sum(x * x, axis=-1, keepdims=True) + NORM_EPS)

def partial_rope(x, pos):
    half = ROPE_DIM // 2
    inv_freq = jnp.power(ROPE_THETA, -jnp.arange(0, ROPE_DIM, 2, dtype=jnp.float32) / ROPE_DIM)
    ang = pos.astype(jnp.float32)[:, None] * inv_freq[None, :]
    cos = jnp.cos(ang)[None, :, None, :]
    sin = jnp.sin(ang)[None, :, None, :]
    xr = x[..., :ROPE_DIM].astype(jnp.float32)
    x1, x2 = xr[..., :half], xr[..., half:]
    rot = jnp.concatenate([x1 * cos - x2 * sin, x2 * cos + x1 * sin], axis=-1).astype(x.dtype)
    return jnp.concatenate([rot, x[..., ROPE_DIM:]], axis=-1)

def moba_attention(q, k, v):
    B, S, H, d = q.shape
    nb = -(-S // MOBA_BLOCK)
    pad = nb * MOBA_BLOCK - S
    nq = S // MOBA_QCHUNK
    topk = min(MOBA_TOPK, nb)
    scale = d ** -0.5
    qh = q.transpose(0, 2, 1, 3)
    kh = jnp.pad(k.transpose(0, 2, 1, 3), ((0, 0), (0, 0), (0, pad), (0, 0)))
    vh = jnp.pad(v.transpose(0, 2, 1, 3), ((0, 0), (0, 0), (0, pad), (0, 0)))
    kb = kh.reshape(B, H, nb, MOBA_BLOCK, d)
    vb = vh.reshape(B, H, nb, MOBA_BLOCK, d)
    k_mean = jnp.mean(kb.astype(jnp.float32), axis=3)
    blk_ids = jnp.arange(nb)
    h_ids = jnp.arange(H)[:, None, None]

    def one_chunk(i):
        b = i // nq
        start = (i % nq) * MOBA_QCHUNK
        qc = lax.dynamic_slice_in_dim(lax.dynamic_index_in_dim(qh, b, 0, keepdims=False),
                                      start, MOBA_QCHUNK, axis=1)
        kb_b = lax.dynamic_index_in_dim(kb, b, 0, keepdims=False)
        vb_b = lax.dynamic_index_in_dim(vb, b, 0, keepdims=False)
        km_b = lax.dynamic_index_in_dim(k_mean, b, 0, keepdims=False)
        own = start // MOBA_BLOCK
        q_pos = start + jnp.arange(MOBA_QCHUNK)
        gate = jnp.einsum('hqd,hnd->hqn', qc.astype(jnp.float32), km_b)
        gate = jnp.where(blk_ids < own, gate, NEG_INF)
        _, sel = lax.top_k(gate, topk)
        sel_ok = sel < own
        k_sel = kb_b[h_ids, sel]
        v_sel = vb_b[h_ids, sel]
        s_sel = jnp.einsum('hqd,hqnkd->hqnk', qc, k_sel).astype(jnp.float32) * scale
        s_sel = jnp.where(sel_ok[..., None], s_sel, NEG_INF).reshape(H, MOBA_QCHUNK, topk * MOBA_BLOCK)
        k_own = lax.dynamic_index_in_dim(kb_b, own, 1, keepdims=False)
        v_own = lax.dynamic_index_in_dim(vb_b, own, 1, keepdims=False)
        k_pos = own * MOBA_BLOCK + jnp.arange(MOBA_BLOCK)
        s_own = jnp.einsum('hqd,hkd->hqk', qc, k_own).astype(jnp.float32) * scale
        s_own = jnp.where(k_pos[None, None, :] <= q_pos[None, :, None], s_own, NEG_INF)
        p = jax.nn.softmax(jnp.concatenate([s_sel, s_own], axis=-1), axis=-1).astype(v.dtype)
        p_sel = p[..., :topk * MOBA_BLOCK].reshape(H, MOBA_QCHUNK, topk, MOBA_BLOCK)
        p_own = p[..., topk * MOBA_BLOCK:]
        return (jnp.einsum('hqnk,hqnkd->hqd', p_sel, v_sel)
                + jnp.einsum('hqk,hkd->hqd', p_own, v_own))

    o = lax.map(one_chunk, jnp.arange(B * nq))
    return o.reshape(B, nq, H, MOBA_QCHUNK, d).transpose(0, 1, 3, 2, 4).reshape(B, S, H, d)

def short_conv(x, w):
    y = lax.conv_general_dilated(x, w[:, None, :].astype(x.dtype), window_strides=(1,),
                                 padding=((DN_CONV - 1, 0),),
                                 dimension_numbers=('NWC', 'WIO', 'NWC'),
                                 feature_group_count=x.shape[-1])
    return jax.nn.silu(y)

def gated_delta_rule(q, k, v, g, beta):
    B, S, H, dk = q.shape
    dv = v.shape[-1]
    out_dtype = v.dtype
    N, C = S // DN_CHUNK, DN_CHUNK
    f32 = jnp.float32
    q = l2norm(q.astype(f32)) * (dk ** -0.5)
    k = l2norm(k.astype(f32))
    v = v.astype(f32)
    to_chunks = lambda t: t.reshape(B, N, C, H, -1).transpose(0, 3, 1, 2, 4)
    q, k, v = to_chunks(q), to_chunks(k), to_chunks(v)
    g = g.astype(f32).reshape(B, N, C, H).transpose(0, 3, 1, 2)
    beta = beta.astype(f32).reshape(B, N, C, H).transpose(0, 3, 1, 2)
    G = jnp.cumsum(g, axis=-1)
    tri = jnp.tril(jnp.ones((C, C), dtype=bool))
    tri_strict = jnp.tril(jnp.ones((C, C), dtype=bool), -1)
    diff = G[..., :, None] - G[..., None, :]
    decay = jnp.where(tri, jnp.exp(jnp.where(tri, diff, 0.0)), 0.0)
    decay_strict = jnp.where(tri_strict, decay, 0.0)
    kb = k * beta[..., None]
    A = jnp.einsum('bhnid,bhnjd->bhnij', kb, k) * decay_strict
    sys = A + jnp.eye(C, dtype=f32)
    u = lax.linalg.triangular_solve(sys, v * beta[..., None], left_side=True, lower=True, unit_diagonal=True)
    w = lax.linalg.triangular_solve(sys, kb * jnp.exp(G)[..., None], left_side=True, lower=True, unit_diagonal=True)
    qk = jnp.einsum('bhnid,bhnjd->bhnij', q, k) * decay
    q_dec = q * jnp.exp(G)[..., None]
    k_dec = k * jnp.exp(G[..., -1:] - G)[..., None]
    g_last = jnp.exp(G[..., -1])

    def step(state, xs):
        q_c, k_c, u_c, w_c, qk_c, gl = xs
        v_new = u_c - jnp.einsum('bhcd,bhde->bhce', w_c, state)
        o = jnp.einsum('bhcd,bhde->bhce', q_c, state) + jnp.einsum('bhij,bhje->bhie', qk_c, v_new)
        state = state * gl[..., None, None] + jnp.einsum('bhcd,bhce->bhde', k_c, v_new)
        return state, o

    xs = tuple(jnp.moveaxis(t, 2, 0) for t in (q_dec, k_dec, u, w, qk, g_last))
    s0 = jnp.zeros((B, H, dk, dv), f32)
    _, o = lax.scan(step, s0, xs)
    return o.transpose(1, 0, 3, 2, 4).reshape(B, S, H, dv).astype(out_dtype)

def setup_inputs(seed: int = 0) -> dict:
    key = jax.random.key(seed)
    ks = jax.random.split(key, 12)
    f32 = jnp.float32
    nrm = lambda k_, shape: jax.random.normal(k_, shape, f32)
    x = nrm(ks[0], (BATCH, SEQ, D_MODEL))
    c = nrm(ks[1], (BATCH, D_MODEL))
    ada_w = nrm(ks[2], (DEPTH, D_MODEL, 3 * D_MODEL)) * (0.5 * D_MODEL ** -0.5)
    ada_b = 0.01 * nrm(ks[3], (DEPTH, 3 * D_MODEL))
    pre_norm_w = 1.0 + 0.02 * nrm(ks[4], (DEPTH, D_MODEL))
    post_norm_w = 1.0 + 0.02 * nrm(ks[5], (DEPTH, D_MODEL))
    w_in = nrm(ks[6], (DEPTH, D_MODEL, D_IN)) * D_MODEL ** -0.5
    conv_w = nrm(ks[7], (DEPTH, DN_CONV, DN_CONV_CH)) * DN_CONV ** -0.5
    a_log = jnp.log(jax.random.uniform(ks[8], (DEPTH, DN_HEADS), f32, 1.0, 16.0))
    dt = jnp.exp(jax.random.uniform(ks[9], (DEPTH, DN_HEADS), f32, math.log(0.001), math.log(0.1)))
    dt_bias = dt + jnp.log(-jnp.expm1(-dt))
    dn_norm_w = 1.0 + 0.02 * nrm(ks[10], (DEPTH, DN_VAL_DIM))
    w_out = nrm(ks[11], (DEPTH, D_MIX, D_MODEL)) * D_MIX ** -0.5
    return {"x": x, "c": c, "ada_w": ada_w, "ada_b": ada_b, "pre_norm_w": pre_norm_w,
            "post_norm_w": post_norm_w, "w_in": w_in, "conv_w": conv_w, "a_log": a_log,
            "dt_bias": dt_bias, "dn_norm_w": dn_norm_w, "w_out": w_out}

def reference(x, c, ada_w, ada_b, pre_norm_w, post_norm_w, w_in, conv_w, a_log, dt_bias, dn_norm_w, w_out):
    B, S, _ = x.shape
    pos = jnp.arange(S, dtype=jnp.int32)
    split_pts = [int(p) for p in np.cumsum(IN_SPLITS)[:-1]]
    for l in range(DEPTH):
        mod = jax.nn.silu(c) @ ada_w[l] + ada_b[l]
        shift, scale, gate = jnp.split(mod, 3, axis=-1)
        h = rmsnorm(x, pre_norm_w[l]) * (1.0 + scale[:, None, :]) + shift[:, None, :]
        proj = h @ w_in[l]
        mq, mk, mv, mg, dq, dk, dv, dz, db, da = jnp.split(proj, split_pts, axis=-1)
        mq = partial_rope(mq.reshape(B, S, MOBA_HEADS, MOBA_HEAD_DIM), pos)
        mk = partial_rope(mk.reshape(B, S, MOBA_HEADS, MOBA_HEAD_DIM), pos)
        mv = mv.reshape(B, S, MOBA_HEADS, MOBA_HEAD_DIM)
        o_moba = moba_attention(mq, mk, mv).reshape(B, S, MOBA_WIDTH) * jax.nn.silu(mg)
        qkv = short_conv(jnp.concatenate([dq, dk, dv], axis=-1), conv_w[l])
        dq, dk, dv = jnp.split(qkv, [DN_QK_WIDTH, 2 * DN_QK_WIDTH], axis=-1)
        g = -jnp.exp(a_log[l].astype(jnp.float32)) * jax.nn.softplus(
            da.astype(jnp.float32) + dt_bias[l].astype(jnp.float32))
        beta = jax.nn.sigmoid(db.astype(jnp.float32))
        o_dn = gated_delta_rule(dq.reshape(B, S, DN_HEADS, DN_KEY_DIM),
                                dk.reshape(B, S, DN_HEADS, DN_KEY_DIM),
                                dv.reshape(B, S, DN_HEADS, DN_VAL_DIM), g, beta)
        o_dn = rmsnorm(o_dn, dn_norm_w[l]).reshape(B, S, DN_WIDTH) * jax.nn.silu(dz)
        y = jnp.concatenate([o_moba, o_dn], axis=-1) @ w_out[l]
        x = x + gate[:, None, :] * rmsnorm(y, post_norm_w[l])
    return x


_drawn_inputs = setup_inputs


def setup_inputs(seed=0):
    import zlib

    import numpy as np

    out = dict(_drawn_inputs(seed))
    spreads = {}
    factors = {'ada_b': 4.716, 'pre_norm_w': 6.122, 'post_norm_w': 22.603, 'dn_norm_w': 27.97}
    for name, (base, spread) in spreads.items():
        noise = np.random.default_rng([zlib.crc32(name.encode()), seed]).standard_normal(out[name].shape)
        drawn = base * np.exp(spread * noise) if base else spread * noise
        out[name] = __import__('jax').numpy.asarray(drawn.astype(out[name].dtype))
    for name, factor in factors.items():
        out[name] = (out[name] * factor).astype(out[name].dtype)
    return out
```

```python
from contextlib import ExitStack

import numpy as np

import concourse.bass as bass
from concourse import mybir

F32 = mybir.dt.float32
F32R = mybir.dt.float32r
ACT = mybir.ActivationFunctionType
ALU = mybir.AluOpType
AX = mybir.AxisListType

P = 128
D = 1024
S = 256
NT = S // P
NK = D // P
AH, AD = 8, 64
AW = AH * AD
DH, DK = 4, 128
DW = DH * DK
CHUNK = 64
NCH = S // CHUNK
EPS = 1e-6
NTH = NT * DH

MQ, MK, MV, MG = 0, AW, 2 * AW, 3 * AW
DQ, DZ, DBA = 4 * AW, 4 * AW + 3 * DW, 4 * AW + 4 * DW
NQKV = 3 * DW // P

R_C, R_SHIFT, R_SCALE, R_PRE, R_DNW, R_CONV = 0, 8, 16, 24, 32, 33
NROWS = R_CONV + 4 * NQKV

LEVELS = 6
C_COS, C_SIN, C_ID, C_TRI, C_CHK, C_MA, C_MQ, C_CM, C_LV = 0, 256, 512, 640, 768, 896, 1024, 1152, 1408
NCONST = C_LV + LEVELS * P

UNIT = 1024
RAW = 5
SPL = 4
N1 = 2 * NK
N2 = 20
N3 = NK
HQ = 3 * DW // 2
GROUPS = [MQ, MK, MG, MV, MQ + 256, MK + 256, MV + 256, MG + 256, DZ, DZ + 256]


def build(nc, x, c, ada_w, ada_b, pre_w, post_w, w_in, conv_w, a_log, dt_bias, dnw, w_out, const, out):
    with ExitStack() as ctx:
        def sb(name, shape, dt=F32, into=ctx):
            return into.enter_context(nc.sbuf_tensor(name, shape, dt))

        def sem(name):
            return ctx.enter_context(nc.semaphore(name))

        bank = [ctx.enter_context(nc.psum_tensor(f"bank{b}", [P, 512], F32)) for b in range(8)]

        cst = sb("cst", [P, NCONST])
        ident = cst[:, C_ID:C_ID + P]
        pcol = sb("pcol", [P, NROWS])
        convh = sb("convh", [P, 4 * NQKV])
        dnwh = sb("dnwh", [P, 1])
        ones = sb("ones", [P, P])
        epsc = sb("epsc", [P, 2])
        sml = sb("sml", [P, 64])
        dab = sb("dab", [P, 8])
        mod_a = sb("mod_a", [P, NK])
        mod_b = sb("mod_b", [P, NK])
        zz = sb("zz", [P, 6, NTH])
        lsq = sb("lsq", [P, 2, NTH])
        gcs = sb("gcs", [P, 4 * NTH])
        cols = sb("cols", [P, 8, NTH])
        ecol = sb("ecol", [P, 3, NTH])
        glx = sb("glx", [P, NCH * DH])
        stat = sb("stat", [P, 96])
        wba = sb("wba", [P, NK, 8])
        hhi = sb("hhi", [P, NK, S], F32R)
        hlo = sb("hlo", [P, NK, S], F32R)
        raw = sb("raw", [P, RAW, UNIT])
        whi = sb("whi", [P, SPL, UNIT], F32R)
        wlo = sb("wlo", [P, SPL, UNIT], F32R)
        accg = sb("accg", [P, D])
        th = sb("th", [P, 2, 512])
        prow = th[:, 0, 0:P]
        qT = sb("qT", [P, 4, S])
        kT = sb("kT", [P, 4, S])
        vt = sb("vt", [P, NT, AW])
        gm = sb("gm", [P, 4, S])
        gz = sb("gz", [P, 4, S])
        stg = sb("stg", [P, 2, 512])

        with ExitStack() as e:
            ada0 = sb("ada0", [P, NK, 512], into=e)
        with ExitStack() as e:
            xres = sb("xres", [P, NT, D], into=e)
            outb = sb("outb", [P, NT, D], into=e)
        sb("hold_ada0", [P, NK * 512])
        with ExitStack() as e:
            qkvs = sb("qkvs", [P, NQKV, S], into=e)
            acc = sb("acc", [P, 2, 512], into=e)
        with ExitStack() as e:
            ohi = sb("ohi", [P, NK, S], F32R, into=e)
            olo = sb("olo", [P, NK, S], F32R, into=e)
        sb("hold_qkvs", [P, NQKV * S + 1024])
        rot = sb("rot", [P, 3, 512])
        pr, pT = sb("pr", [P, 2, 384]), sb("pT", [P, 2, 384])
        with ExitStack() as e:
            xs = sb("xs", [P, NT, D], into=e)
            xT = xs[:, :, :].rearrange("p t (k s) -> p (t k) s", s=S)
            xn = sb("xn", [P, NT, D], into=e)
            ada1 = sb("ada1", [P, NK, 512], into=e)
            hT = sb("hT", [P, NK, S], into=e)
            cv = sb("cv", [P, NQKV, S], into=e)
        def th_array(name):
            return sb(name, [P, NTH, P])
        kw, kd, vb = th_array("kw"), th_array("kd"), th_array("vb")
        dec = sb("dec", [P, 2, NTH, P])
        am, qkd, qd = th_array("am"), th_array("qkd"), th_array("qd")
        ti, tt = th_array("ti"), th_array("tt")
        zt, ml = th_array("zt"), th_array("ml")
        wT, vnew = zt, kw
        state = sb("state", [P, DH, P])
        on = sb("on", [P, DH, P])
        ada = [ada0, ada1]
        sq = dec[:, :, :, :].rearrange("p a b c -> p (a b c)").rearrange("p (i s) -> p i s", s=S)

        prow_loaded, const_loaded, level_loaded, dab_loaded, wba_loaded = map(
            sem, ("prow_loaded", "const_loaded", "level_loaded", "dab_loaded", "wba_loaded"))
        gbias_loaded, postw_loaded, xres_loaded, stored = map(sem, ("gbias_loaded", "postw_loaded", "xres_loaded", "stored"))
        x_loaded = [sem(f"x_loaded{t}") for t in range(NT)]
        ada_loaded = [[sem(f"ada_loaded{s}{h}") for h in range(2)] for s in range(2)]
        raw_loaded = [sem(f"raw_loaded{s}") for s in range(RAW)]
        dve_step, act_step = sem("dve_step"), sem("act_step")
        pool_init, dve_init, prow_turned, pcol_done, c_tanh, sc_done, xms_done, xn_done, xT_ready, xT_done, expa_done = map(
            sem, ("pool_init", "dve_init", "prow_turned", "pcol_done", "c_tanh", "sc_done", "xms_done", "xn_done", "xT_ready",
                  "xT_done", "expa_done"))
        acc_done, mod_ready, mod_read, h_done, hhi_done, hlo_done = map(
            sem, ("acc_done", "mod_ready", "mod_read", "h_done", "hhi_done", "hlo_done"))
        hi_done, lo_done, unit_done, group_ready = map(sem, ("hi_done", "lo_done", "unit_done", "group_ready"))
        qkv_ready, tap_done, conv_done, ctanh_done, silu_done, sq_done = map(
            sem, ("qkv_ready", "tap_done", "conv_done", "ctanh_done", "silu_done", "sq_done"))
        ba_ready, ba_abs, ba_ln, g_done, cum_ready, cum_copied, ssq_ready, lsq_done, cols_done, ecol_done = map(
            sem, ("ba_ready", "ba_abs", "ba_ln", "g_done", "cum_ready", "cum_copied", "ssq_ready", "lsq_done", "cols_done",
                  "ecol_done"))
        rows_ready, rows_exp, row_sums, dec_done, kk_ready, a_done, ktok_ready, ktok_used, vtok_ready, vtok_used, qd_done = map(
            sem, ("rows_ready", "rows_exp", "row_sums", "dec_done", "kk_ready", "a_done", "ktok_ready", "ktok_used",
                  "vtok_ready", "vtok_used", "qd_done"))
        ml_done, z_ready, z_copied, x_ready, t_done, wT_ready, wT_copied = map(
            sem, ("ml_done", "z_ready", "z_copied", "x_ready", "t_done", "wT_ready", "wT_copied"))
        vnew_ready, vnew_copied, state_ready, state_done, o_ready, osq_done, oss_done, orstd_done, on_done = map(
            sem, ("vnew_ready", "vnew_copied", "state_ready", "state_done", "o_ready", "osq_done", "oss_done", "orstd_done",
                  "on_done"))
        oT_ready, odn_done, odn_hi, odn_split = map(sem, ("oT_ready", "odn_done", "odn_hi", "odn_split"))
        shuffled, times_sin, rope_done, v_copied, gtanh_done, gate_done = map(
            sem, ("shuffled", "times_sin", "rope_done", "v_copied", "gtanh_done", "gate_done"))
        s_ready, nmax_done, p_done, pn_done, pT_ready, pT_copied, pv_ready, oa_done, oa_hi, oa_split = map(
            sem, ("s_ready", "nmax_done", "p_done", "pn_done", "pT_ready", "pT_copied", "pv_ready", "oa_done", "oa_hi",
                  "oa_split"))
        gate_acc, gate_ready, gp_done, y_ready, ysq_done, ysum_done, yrstd_done, y_done = map(
            sem, ("gate_acc", "gate_ready", "gp_done", "y_ready", "ysq_done", "ysum_done", "yrstd_done", "y_done"))

        def raw_u(n):
            return raw[:, n % RAW, 0:(HQ if n < N1 else UNIT)]

        def split_u(buf, n):
            return buf[:, n % SPL, 0:(HQ if n < N1 else UNIT)]

        def four(b):
            return bank[b][:, :].rearrange("p (h j) -> p h j", h=4)

        def two(b):
            return bank[b][:, :].rearrange("p (a s) -> p a s", a=2)

        def heads(a, t):
            return a[:, t * DH:(t + 1) * DH, :]

        def over_heads(col):
            return cst[:, col:col + P].unsqueeze(1).to_broadcast([P, DH, P])

        def over_cols(ap):
            return ap.unsqueeze(2).to_broadcast([P, DH, P])

        BULK, ATT, YB = [7, 0], [1, 6], [[7, 0], [1, 6]]
        GQK = {0: (qT, 0), 1: (kT, 0), 4: (qT, 2), 5: (kT, 2)}
        GV = {3: 0, 6: 1}
        GG = {2: (gm, 0), 7: (gm, 2), 8: (gz, 0), 9: (gz, 2)}
        ROPES, VS, GATES = sorted(GQK), sorted(GV), sorted(GG)
        QKV_ORDER = [4, 5, 6, 7, 0, 1, 2, 3, 8, 9, 10, 11]
        PAIRS = QKV_ORDER[::2]

        def bank_of_group(u):
            return BULK[u % 2]

        def used_up(n):
            if n < N1 - 2:
                return unit_done, n + 1
            if n < N1:
                return qkv_ready, len(PAIRS)
            j = n - N1
            if j < N2:
                return (unit_done, N1 - 2 + j // 2 + 1) if j % 2 == 0 else (group_ready, j // 2 + 1)
            return unit_done, N1 - 2 + N2 // 2 + j - N2 + 1

        block = ctx.enter_context(nc.Block())

        @block.sync
        def _(sp):
            for r0, n, src in ((R_C, 8, c.rearrange("a (r p) -> (a r) p", p=P)),
                               (R_SHIFT, 16, ada_b[:, 0:2 * D].rearrange("a (r p) -> (a r) p", p=P)),
                               (R_PRE, 8, pre_w.rearrange("a (r p) -> (a r) p", p=P)),
                               (R_DNW, 1, dnw),
                               (R_CONV, 4 * NQKV, conv_w.rearrange("a j (i p) -> (a j i) p", p=P))):
                sp.dma_start(prow[r0:r0 + n, :], src).then_inc(prow_loaded, 16)
            sp.dma_start(cst[:, 0:C_LV], const[:, 0:C_LV]).then_inc(const_loaded, 16)
            for t in range(NT):
                sp.dma_start(xs[:, t, :], x[0, t * P:(t + 1) * P, :]).then_inc(x_loaded[t], 16)

            def load_ada(q):
                if q >= 2:
                    sp.wait_ge(acc_done, q - 1)
                for hf in range(2):
                    for part in range(2):
                        src = ada_w[0, 4 * hf * P:(4 * hf + 4) * P, part * D + q * 256:part * D + (q + 1) * 256]
                        sp.dma_start(ada[q % 2][:, 4 * hf:4 * hf + 4, part * 256:(part + 1) * 256],
                                     src.rearrange("(k p) n -> p k n", p=P)).then_inc(ada_loaded[q % 2][hf], 16)

            def load_unit(n):
                if n >= RAW:
                    sp.wait_ge(lo_done, n - RAW + 1)
                if n < N1:
                    k, hf = n // 2, n % 2
                    src, dst = w_in[0, k * P:(k + 1) * P, DQ + hf * HQ:DQ + (hf + 1) * HQ], raw_u(n)
                elif n < N1 + N2:
                    u, hf = (n - N1) // 2, (n - N1) % 2
                    src = w_in[0, hf * 4 * P:(hf + 1) * 4 * P, GROUPS[u]:GROUPS[u] + 256].rearrange("(k p) n -> p k n", p=P)
                    dst = raw_u(n).rearrange("p (k n) -> p k n", k=4)
                else:
                    k = n - N1 - N2
                    src, dst = w_out[0, k * P:(k + 1) * P, :], raw_u(n)
                sp.dma_start(dst, src).then_inc(raw_loaded[n % RAW], 16)

            def load_gate(i):
                if i == 0:
                    sp.wait_ge(acc_done, 3)
                else:
                    sp.wait_ge(gate_acc, NK)
                for hf in range(2):
                    src = ada_w[0, 4 * hf * P:(4 * hf + 4) * P, 2 * D + i * 512:2 * D + (i + 1) * 512]
                    sp.dma_start(ada0[:, 4 * hf:4 * hf + 4, :],
                                 src.rearrange("(k p) n -> p k n", p=P)).then_inc(ada_loaded[0][hf], 16)

            load_ada(0)
            load_ada(1)
            for n in range(0, 4):
                load_unit(n)
            load_ada(2)
            for n in range(4, 8):
                load_unit(n)
            load_ada(3)
            sp.dma_start(dab[:, 0:4], dt_bias[0].partition_broadcast(P)).then_inc(dab_loaded, 16)
            sp.dma_start(dab[:, 4:8], a_log[0].partition_broadcast(P)).then_inc(dab_loaded, 16)
            sp.dma_start(wba[:, :, :], w_in[0, :, DBA:DBA + 8].rearrange("(k p) n -> p k n", p=P)).then_inc(wba_loaded, 16)
            for n in range(8, N1 + 2):
                load_unit(n)
            sp.dma_start(cst[:, C_LV:], const[:, C_LV:]).then_inc(level_loaded, 16)
            sp.wait_ge(pool_init, 1)
            sp.dma_start(accg[0:1, :], ada_b[:, 2 * D:3 * D]).then_inc(gbias_loaded, 16)
            for n in range(N1 + 2, N1 + 8):
                load_unit(n)
            load_gate(0)
            for n in range(N1 + 8, N1 + 15):
                load_unit(n)
            load_gate(1)
            for n in range(N1 + 15, N1 + N2):
                load_unit(n)
            for n in range(N1 + N2, N1 + N2 + 3):
                load_unit(n)
            sp.wait_ge(gate_acc, 2 * NK)
            sp.dma_start(outb[:, 0, :], post_w[0].partition_broadcast(P)).then_inc(postw_loaded, 16)
            sp.dma_start(xres[:, :, :], x[0].rearrange("(t p) n -> p t n", p=P)).then_inc(xres_loaded, 16)
            for n in range(N1 + N2 + 3, N1 + N2 + N3):
                load_unit(n)
            for t in range(NT):
                for hf in range(2):
                    sp.wait_ge(y_done, 2 * t + hf + 1)
                    sp.dma_start(out[0, t * P:(t + 1) * P, hf * 512:(hf + 1) * 512],
                                 outb[:, t, hf * 512:(hf + 1) * 512]).then_inc(stored, 16)
            sp.wait_ge(stored, 16 * 2 * NT)

        @block.gpsimd
        def _(pool):
            pool.memset(accg[:, :], 0.0).then_inc(pool_init, 1)

            def lo(n):
                pool.wait_ge(hi_done, n + 1)
                pool.tensor_tensor(split_u(wlo, n), raw_u(n), split_u(whi, n).bitcast(F32), ALU.subtract).then_inc(lo_done, 1)

            def level_mask(l):
                for t in range(NT):
                    if l == 0:
                        pool.wait_ge(level_loaded, 16)
                        pool.wait_ge(a_done, 2 * t + 1)
                    else:
                        pool.wait_ge(z_ready, NT * (l - 1) + t + 1)
                        if l == 1:
                            pool.wait_ge(t_done, 2 * t + 2)
                    pool.tensor_tensor(heads(ml, t), heads(am, t), over_heads(C_LV + l * P), ALU.mult).then_inc(ml_done, 1)

            def rope_sin(r):
                pool.wait_ge(shuffled, r + 1)
                if r >= 1:
                    pool.wait_ge(rope_done, r)
                pool.tensor_tensor(rot[:, 1, :].rearrange("p (a s) -> p a s", a=2), rot[:, 0, :].rearrange("p (a s) -> p a s", a=2),
                                   cst[:, C_SIN:C_SIN + S].unsqueeze(1).to_broadcast([P, 2, S]), ALU.mult).then_inc(times_sin, 1)

            for n in range(N1 + 3):
                lo(n)
            for j in range(N2):
                if j in (1, 3, 9, 12):
                    rope_sin((1, 3, 9, 12).index(j))
                if j in (8, 9, 11, 13, 15, 17):
                    level_mask((8, 9, 11, 13, 15, 17).index(j))
                lo(N1 + 3 + j)
            for n in range(N1 + N2 + 3, N1 + N2 + N3):
                lo(n)

        @block.scalar
        def _(act):
            steps = [0]

            def link(ins):
                steps[0] += 1
                ins.then_inc(act_step, 1)
                act.wait_ge(act_step, steps[0])

            def hi(n):
                act.wait_ge(raw_loaded[n % RAW], 16 * (n // RAW + 1))
                if n >= SPL:
                    act.wait_ge(*used_up(n - SPL))
                act.activation(split_u(whi, n), raw_u(n), ACT.Copy).then_inc(hi_done, 1)

            act.wait_ge(pcol_done, 1)
            act.activation(sml[:, 0:8], pcol[:, R_C:R_C + 8], ACT.Tanh, scale=0.5).then_inc(c_tanh, 1)
            for t in range(NT):
                act.wait_ge(x_loaded[t], 16)
                act.activation(xn[:, t, :], xs[:, t, :], ACT.Square, accum_out=sml[:, 16 + t:17 + t]).then_inc(xms_done, 1)
            act.wait_ge(xms_done, 2)
            act.wait_ge(dve_init, 1)
            link(act.activation(sml[:, 18:20], sml[:, 16:18], ACT.Ln, scale=1.0 / D, bias=epsc[:, 0:1]))
            link(act.activation(sml[:, 20:22], sml[:, 18:20], ACT.Exp, scale=-0.5))
            for t in range(NT):
                act.activation(xn[:, t, :], xs[:, t, :], ACT.Copy, scale=sml[:, 20 + t:21 + t]).then_inc(xn_done, 1)
            for b in range(4):
                act.wait_ge(xT_ready, b + 1)
                act.activation(xT[:, 2 * b:2 * b + 2, :], two(b), ACT.Copy).then_inc(xT_done, 1)

            def h_hi(q):
                act.wait_ge(h_done, q + 1)
                act.activation(hhi[:, 2 * q:2 * q + 2, :], hT[:, 2 * q:2 * q + 2, :], ACT.Copy).then_inc(hhi_done, 1)

            h_hi(0)
            h_hi(1)
            for n in range(0, 4):
                hi(n)
            h_hi(2)
            for n in range(4, 8):
                hi(n)
            h_hi(3)
            for n in range(8, N1 + 1):
                hi(n)

            def taps(m):
                act.wait_ge(qkv_ready, m + 1)
                for i in (PAIRS[m], PAIRS[m] + 1):
                    act.activation(cv[:, i, :], bank[i // 2][:, (i % 2) * S:(i % 2 + 1) * S], ACT.Copy,
                                   scale=convh[:, 3 * NQKV + i:3 * NQKV + i + 1]).then_inc(tap_done, 1)

            def conv_tanh(m):
                i = PAIRS[m]
                act.wait_ge(conv_done, m + 1)
                if m >= 2:
                    act.wait_ge(silu_done, m - 1)
                act.activation(th[:, m % 2, :].rearrange("p (a s) -> p a s", a=2), cv[:, i:i + 2, :], ACT.Tanh).then_inc(ctanh_done, 1)

            def squares(m):
                i = PAIRS[m]
                act.wait_ge(silu_done, m + 1)
                act.activation(sq[:, 2 * m:2 * m + 2, :], qkvs[:, i:i + 2, :], ACT.Square).then_inc(sq_done, 1)

            def softplus():
                act.wait_ge(ba_abs, 1)
                link(act.activation(zz[:, 2:4, :], zz[:, 4:6, :], ACT.Exp, scale=-1.0))
                act.activation(zz[:, 4:6, :], zz[:, 2:4, :], ACT.Ln, bias=1.0).then_inc(ba_ln, 1)
                act.wait_ge(dab_loaded, 32)
                act.activation(dab[:, 4:8], dab[:, 4:8], ACT.Exp).then_inc(expa_done, 1)

            def norms():
                act.wait_ge(ssq_ready, 1)
                act.activation(lsq[:, 0, :], bank[6][:, 0:NTH], ACT.Ln, bias=epsc[:, 0:1]).then_inc(lsq_done, 1)
                act.activation(lsq[:, 1, :], bank[6][:, NTH:2 * NTH], ACT.Ln, bias=epsc[:, 1:2], scale=float(DK)).then_inc(lsq_done, 1)

            def factors():
                act.wait_ge(cols_done, 1)
                act.activation(ecol[:, :, :], cols[:, 0:3, :], ACT.Exp).then_inc(ecol_done, 1)
                act.activation(glx[:, :], gcs[:, 2 * NTH:], ACT.Exp).then_inc(ecol_done, 1)

            def decays(t):
                act.wait_ge(rows_ready, t + 1)
                act.activation(heads(qd, t), four(5), ACT.Exp).then_inc(rows_exp, 1)
                for a in range(2):
                    act.wait_ge(row_sums, 2 * t + a + 1)
                    act.activation(heads(dec[:, a, :, :], t), heads(dec[:, a, :, :], t), ACT.Exp).then_inc(dec_done, 1)

            def z_copy(l):
                for t in range(NT):
                    act.wait_ge(z_ready, NT * l + t + 1)
                    if l >= 2:
                        act.wait_ge(x_ready, NT * (l - 2) + t + 1)
                    act.activation(heads(zt, t), four(2 + 2 * t), ACT.Copy).then_inc(z_copied, 1)

            def v_copy(i):
                u = VS[i]
                act.wait_ge(group_ready, u + 1)
                act.activation(vt[:, :, i * 256:(i + 1) * 256], two(bank_of_group(u)), ACT.Copy).then_inc(v_copied, 1)

            def gate_tanh(i):
                u = GATES[i]
                act.wait_ge(group_ready, u + 1)
                act.wait_ge(silu_done, 6)
                if i >= 2:
                    act.wait_ge(gate_done, i - 1)
                act.activation(th[:, i % 2, :], bank[bank_of_group(u)][:, :], ACT.Tanh, scale=0.5).then_inc(gtanh_done, 1)

            def probs(m):
                act.wait_ge(nmax_done, m + 1)
                if m >= 1:
                    act.wait_ge(pT_ready, m)
                for e in range(2):
                    for qt in range(NT):
                        i, o, w = 2 * (2 * m + e) + qt, qt * P, (qt + 1) * P
                        act.activation(pr[:, e, o:o + w], bank[ATT[e]][:, o:o + w], ACT.Exp, scale=AD ** -0.5,
                                       bias=stat[:, 16 + i:17 + i], accum_out=stat[:, 32 + i:33 + i]).then_inc(p_done, 1)

            def pT_copy(m):
                act.wait_ge(pT_ready, m + 1)
                if m >= 1:
                    act.wait_ge(pv_ready, m)
                for e in range(2):
                    act.activation(pT[:, e, :], bank[ATT[e]][:, 0:384], ACT.Copy).then_inc(pT_copied, 1)

            def heads_hi(m):
                act.wait_ge(oa_done, m + 1)
                act.activation(ohi[:, m, :], stg[:, m % 2, 0:S], ACT.Copy).then_inc(oa_hi, 1)

            def wT_copy(t):
                act.wait_ge(wT_ready, t + 1)
                act.activation(heads(wT, t), four(2 + 2 * t), ACT.Copy, scale=-1.0).then_inc(wT_copied, 1)

            def vnew_copy(n):
                act.wait_ge(vnew_ready, n + 1)
                r = slice((n % 2) * CHUNK, (n % 2 + 1) * CHUNK)
                act.activation(heads(vnew, n // 2)[r], four(2)[r], ACT.Copy).then_inc(vnew_copied, 1)

            def o_norm(t):
                act.wait_ge(o_ready, t + 1)
                act.wait_ge(gate_done, 4)
                act.activation(th[:, t, :], bank[4 + t][:, :], ACT.Square).then_inc(osq_done, 1)
                act.wait_ge(oss_done, t + 1)
                link(act.activation(stat[:, 56 + 4 * t:60 + 4 * t], stat[:, 48 + 4 * t:52 + 4 * t], ACT.Ln, scale=1.0 / DK,
                                    bias=epsc[:, 0:1]))
                act.activation(stat[:, 64 + 4 * t:68 + 4 * t], stat[:, 56 + 4 * t:60 + 4 * t], ACT.Exp, scale=-0.5).then_inc(orstd_done, 1)

            def dn_hi(t):
                act.wait_ge(odn_done, t + 1)
                act.activation(ohi[:, 4:8, t * P:(t + 1) * P], stg[:, t, :].rearrange("p (h s) -> p h s", h=4), ACT.Copy).then_inc(odn_hi, 1)

            def y_norm(t):
                act.wait_ge(y_ready, t + 1)
                for hf in range(2):
                    if t >= 1 and hf == 0:
                        act.wait_ge(ysq_done, 2 * t)
                    act.activation(th[:, hf, :], bank[YB[t][hf]][:, :], ACT.Square,
                                   accum_out=sml[:, 40 + 2 * t + hf:41 + 2 * t + hf]).then_inc(ysq_done, 1)
                act.wait_ge(ysum_done, t + 1)
                link(act.activation(sml[:, 46 + t:47 + t], sml[:, 44 + t:45 + t], ACT.Ln, scale=1.0 / D, bias=epsc[:, 0:1]))
                act.activation(sml[:, 48 + t:49 + t], sml[:, 46 + t:47 + t], ACT.Exp, scale=-0.5).then_inc(yrstd_done, 1)

            taps(0)
            taps(1)
            hi(N1 + 1)
            softplus()
            conv_tanh(0)
            taps(2)
            squares(0)
            conv_tanh(1)
            hi(N1 + 2)
            taps(3)
            squares(1)
            conv_tanh(2)
            taps(4)
            hi(N1 + 3)
            squares(2)
            conv_tanh(3)
            taps(5)
            hi(N1 + 4)
            squares(3)
            conv_tanh(4)
            conv_tanh(5)
            hi(N1 + 5)
            norms()
            factors()
            hi(N1 + 6)
            hi(N1 + 7)
            probs(0)
            decays(0)
            hi(N1 + 8)
            gate_tanh(0)
            decays(1)
            hi(N1 + 9)
            pT_copy(0)
            v_copy(0)
            hi(N1 + 10)
            hi(N1 + 11)
            heads_hi(0)
            z_copy(1)
            probs(1)
            hi(N1 + 12)
            hi(N1 + 13)
            pT_copy(1)
            z_copy(2)
            heads_hi(1)
            hi(N1 + 14)
            probs(2)
            hi(N1 + 15)
            v_copy(1)
            pT_copy(2)
            z_copy(3)
            hi(N1 + 16)
            gate_tanh(1)
            hi(N1 + 17)
            heads_hi(2)
            z_copy(4)
            probs(3)
            hi(N1 + 18)
            gate_tanh(2)
            pT_copy(3)
            hi(N1 + 19)
            z_copy(5)
            heads_hi(3)
            hi(N1 + N2)
            gate_tanh(3)
            hi(N1 + N2 + 1)
            wT_copy(0)
            wT_copy(1)
            hi(N1 + N2 + 2)
            vnew_copy(0)
            vnew_copy(1)
            hi(N1 + N2 + 3)
            o_norm(0)
            vnew_copy(2)
            hi(N1 + N2 + 4)
            dn_hi(0)
            vnew_copy(3)
            hi(N1 + N2 + 5)
            o_norm(1)
            hi(N1 + N2 + 6)
            hi(N1 + N2 + 7)
            dn_hi(1)
            y_norm(0)
            y_norm(1)

        @block.vector
        def _(dve):
            steps = [0]

            def link(ins):
                steps[0] += 1
                ins.then_inc(dve_step, 1)
                dve.wait_ge(dve_step, steps[0])

            dve.memset(ones[:, :], 1.0)
            dve.memset(epsc[:, 0:1], EPS)
            dve.memset(epsc[:, 1:2], DK * EPS).then_inc(dve_init, 1)
            dve.wait_ge(prow_turned, 1)
            dve.tensor_copy(pcol[:, :], bank[7][:, 0:NROWS]).then_inc(pcol_done, 1)
            dve.wait_ge(pcol_done, 1)
            dve.tensor_scalar(convh[:, :], pcol[:, R_CONV:], 0.5, None, ALU.mult)
            dve.tensor_scalar(dnwh[:, :], pcol[:, R_DNW:R_DNW + 1], 0.5, None, ALU.mult)
            dve.wait_ge(c_tanh, 1)
            link(dve.scalar_tensor_tensor(sml[:, 8:16], sml[:, 0:8], 1.0, pcol[:, R_C:R_C + 8], ALU.add, ALU.mult))
            dve.tensor_scalar(sml[:, 24:32], sml[:, 8:16], 0.5, None, ALU.mult).then_inc(sc_done, 1)
            dve.wait_ge(sc_done, 1)

            def mod_sums(q):
                a = acc[:, q % 2, :]
                if q >= 2:
                    dve.wait_ge(mod_ready, q - 1)
                for k in range(NK):
                    if k % 4 == 0:
                        dve.wait_ge(ada_loaded[q % 2][k // 4], 32 * (q // 2 + 1))
                    if k == 0:
                        ins = dve.tensor_scalar(a, ada[q % 2][:, k, :], sml[:, 24 + k:25 + k], None, ALU.mult)
                    else:
                        ins = dve.scalar_tensor_tensor(a, ada[q % 2][:, k, :], sml[:, 24 + k:25 + k], a, ALU.mult, ALU.add)
                    if k < NK - 1:
                        link(ins)
                    else:
                        ins.then_inc(acc_done, 1)

            def modulate(q):
                k2, b = slice(2 * q, 2 * q + 2), bank[6 + q % 2]
                dve.wait_ge(mod_ready, q + 1)
                dve.tensor_tensor(mod_b[:, k2], b[:, 0:2], pcol[:, R_SHIFT + 2 * q:R_SHIFT + 2 * q + 2], ALU.add)
                link(dve.tensor_tensor(sml[:, 32:34], b[:, 2:4], pcol[:, R_SCALE + 2 * q:R_SCALE + 2 * q + 2], ALU.add))
                dve.scalar_tensor_tensor(mod_a[:, k2], sml[:, 32:34], 1.0, pcol[:, R_PRE + 2 * q:R_PRE + 2 * q + 2],
                                         ALU.add, ALU.mult).then_inc(mod_read, 1)
                dve.wait_ge(mod_read, q + 1)
                dve.wait_ge(xT_done, q + 1)
                for k in (2 * q, 2 * q + 1):
                    ins = dve.tensor_scalar(hT[:, k, :], xT[:, k, :], mod_a[:, k:k + 1], mod_b[:, k:k + 1], ALU.mult, ALU.add)
                ins.then_inc(h_done, 1)
                dve.wait_ge(hhi_done, q + 1)
                dve.tensor_tensor(hlo[:, k2, :], hT[:, k2, :], hhi[:, k2, :].bitcast(F32), ALU.subtract).then_inc(hlo_done, 1)

            for q in range(4):
                mod_sums(q)
                modulate(q)

            def conv(m):
                for i in (PAIRS[m], PAIRS[m] + 1):
                    b = bank[i // 2][:, (i % 2) * S:(i % 2 + 1) * S]
                    dve.wait_ge(tap_done, 2 * m + 2)
                    for j in range(1, 4):
                        w = convh[:, (3 - j) * NQKV + i:(3 - j) * NQKV + i + 1]
                        ins = dve.scalar_tensor_tensor(cv[:, i, j:], b[:, 0:S - j], w, cv[:, i, j:], ALU.mult, ALU.add)
                        if j < 3 or i == PAIRS[m]:
                            link(ins)
                ins.then_inc(conv_done, 1)

            def conv_silu(m):
                i = PAIRS[m]
                dve.wait_ge(ctanh_done, m + 1)
                dve.scalar_tensor_tensor(qkvs[:, i:i + 2, :], th[:, m % 2, :].rearrange("p (a s) -> p a s", a=2), 1.0, cv[:, i:i + 2, :],
                                         ALU.add, ALU.mult).then_inc(silu_done, 1)

            def gates_in():
                ba = bank[6][:, 0:16].rearrange("p (t n) -> p t n", t=NT)
                z = [zz[:, a, :].rearrange("p (t h) -> p t h", t=NT) for a in range(2)]
                dve.wait_ge(ba_ready, 1)
                dve.wait_ge(dab_loaded, 32)
                dve.tensor_scalar(z[0], ba[:, :, 0:4], -1.0, None, ALU.mult)
                link(dve.tensor_tensor(z[1], ba[:, :, 4:8], dab[:, 0:4].unsqueeze(1).to_broadcast([P, NT, DH]), ALU.add))
                dve.scalar_tensor_tensor(zz[:, 4:6, :], zz[:, 0:2, :], -1.0, zz[:, 0:2, :], ALU.mult, ALU.max).then_inc(ba_abs, 1)

            def gates_out():
                dve.wait_ge(ba_ln, 1)
                link(dve.scalar_tensor_tensor(zz[:, 2:4, :], zz[:, 0:2, :], 0.0, zz[:, 4:6, :], ALU.max, ALU.add))
                dve.tensor_scalar(cols[:, 2, :], zz[:, 2, :], -1.0, None, ALU.mult)
                dve.wait_ge(expa_done, 1)
                dve.scalar_tensor_tensor(zz[:, 0, :].rearrange("p (t h) -> p t h", t=NT), zz[:, 3, :].rearrange("p (t h) -> p t h", t=NT), -1.0,
                                         dab[:, 4:8].unsqueeze(1).to_broadcast([P, NT, DH]), ALU.mult, ALU.mult).then_inc(g_done, 1)

            def cum_copy():
                dve.wait_ge(cum_ready, 1)
                dve.tensor_copy(gcs[:, :], bank[6][:, 0:4 * NTH]).then_inc(cum_copied, 1)

            def columns():
                g, gl, lk, lq, lb = gcs[:, 0:NTH], gcs[:, NTH:2 * NTH], lsq[:, 0, :], lsq[:, 1, :], cols[:, 2, :]
                dve.wait_ge(cum_copied, 1)
                dve.wait_ge(lsq_done, 2)
                dve.scalar_tensor_tensor(cols[:, 3, :], lk, 0.5, g, ALU.mult, ALU.add)
                dve.scalar_tensor_tensor(cols[:, 4, :], lq, -0.5, g, ALU.mult, ALU.add)
                dve.scalar_tensor_tensor(cols[:, 5, :], lk, -0.5, lb, ALU.mult, ALU.add)
                link(dve.scalar_tensor_tensor(cols[:, 6, :], lk, -0.5, gl, ALU.mult, ALU.add))
                dve.tensor_tensor(cols[:, 0, :], cols[:, 5, :], g, ALU.add)
                dve.tensor_tensor(cols[:, 1, :], cols[:, 6, :], g, ALU.subtract).then_inc(cols_done, 1)

            def k_tokens(t):
                dve.wait_ge(ktok_ready, t + 1)
                dve.wait_ge(ecol_done, 2)
                dve.tensor_tensor(heads(kw, t), four(2 + t), over_cols(ecol[:, 0, t * DH:(t + 1) * DH]), ALU.mult)
                dve.tensor_tensor(heads(kd, t), four(2 + t), over_cols(ecol[:, 1, t * DH:(t + 1) * DH]), ALU.mult).then_inc(ktok_used, 1)

            def v_tokens(t):
                dve.wait_ge(vtok_ready, t + 1)
                dve.tensor_tensor(heads(vb, t), four(4 + t), over_cols(ecol[:, 2, t * DH:(t + 1) * DH]), ALU.mult).then_inc(vtok_used, 1)

            def row_sum(t):
                dve.wait_ge(rows_ready, t + 1)
                dve.wait_ge(ssq_ready, 1)
                for a, b, col, mask, rev in ((0, 4, 0, C_MA, True), (1, 5, 3, C_MQ, False)):
                    if a == 1:
                        dve.wait_ge(rows_exp, t + 1)
                    for h in range(DH):
                        i = t * DH + h
                        ins = dve.scalar_tensor_tensor(dec[:, a, i, :], four(b)[:, h, :], cols[:, col, i:i + 1], cst[:, mask:mask + P],
                                                       ALU.subtract, ALU.min, reverse0=rev)
                    ins.then_inc(row_sums, 1)

            def decayed(t):
                dve.wait_ge(kk_ready, t + 1)
                dve.wait_ge(dec_done, 2 * t + 2)
                dve.tensor_tensor(heads(am, t), four(2), heads(dec[:, 0, :, :], t), ALU.mult).then_inc(a_done, 1)
                dve.tensor_tensor(heads(qkd, t), four(3), heads(dec[:, 1, :, :], t), ALU.mult).then_inc(a_done, 1)
                dve.wait_ge(rows_exp, t + 1)
                dve.tensor_tensor(heads(qd, t), heads(qd, t), qkvs[:, 0:4, t * P:(t + 1) * P], ALU.mult).then_inc(qd_done, 1)

            def first_inverse():
                for t in range(NT):
                    dve.wait_ge(z_ready, t + 1)
                    dve.tensor_tensor(heads(tt, t), over_heads(C_ID), four(2 + 2 * t), ALU.subtract).then_inc(t_done, 1)
                    dve.wait_ge(ml_done, t + 1)
                    dve.tensor_tensor(heads(ti, t), over_heads(C_ID), heads(ml, t), ALU.subtract).then_inc(t_done, 1)

            def merge(l):
                for t in range(NT):
                    dve.wait_ge(x_ready, NT * (l - 1) + t + 1)
                    if l < LEVELS - 1:
                        dve.tensor_tensor(heads(ti, t), heads(ti, t), four(3 + 2 * t), ALU.subtract)
                    dve.tensor_tensor(heads(tt, t), heads(tt, t), four(2 + 2 * t), ALU.subtract).then_inc(t_done, 1)

            def rope(r):
                u = ROPES[r]
                dst, i = GQK[u]
                dve.wait_ge(group_ready, u + 1)
                if r >= 1:
                    dve.wait_ge(times_sin, r)
                dve.stream_shuffle(rot[:, 0, :], bank[bank_of_group(u)][:, :], [p ^ 8 if p < 16 else p for p in range(32)]).then_inc(shuffled, 1)
                link(dve.tensor_tensor(rot[:, 2, :].rearrange("p (a s) -> p a s", a=2), two(bank_of_group(u)),
                                       cst[:, C_COS:C_COS + S].unsqueeze(1).to_broadcast([P, 2, S]), ALU.mult))
                dve.wait_ge(times_sin, r + 1)
                dve.tensor_tensor(dst[:, i:i + 2, :], rot[:, 1, :].rearrange("p (a s) -> p a s", a=2),
                                  rot[:, 2, :].rearrange("p (a s) -> p a s", a=2), ALU.add).then_inc(rope_done, 1)

            def gate(i):
                u = GATES[i]
                dst, j = GG[u]
                dve.wait_ge(gtanh_done, i + 1)
                dve.scalar_tensor_tensor(dst[:, j:j + 2, :], th[:, i % 2, :].rearrange("p (a s) -> p a s", a=2), 1.0, two(bank_of_group(u)),
                                         ALU.add, ALU.mult).then_inc(gate_done, 1)

            def maxima(m):
                dve.wait_ge(s_ready, m + 1)
                for e in range(2):
                    for qt in range(NT):
                        i, o, w = 2 * (2 * m + e) + qt, qt * P, (qt + 1) * P
                        s = bank[ATT[e]][:, o:o + w]
                        ins = dve.tensor_tensor_reduce(s, s, cst[:, C_CM + 2 * P - w:C_CM + 2 * P], 1.0, -3e38, ALU.add, ALU.max,
                                                       stat[:, i:i + 1])
                link(ins)
                dve.tensor_scalar(stat[:, 16 + 4 * m:20 + 4 * m], stat[:, 4 * m:4 * m + 4], -(AD ** -0.5), None, ALU.mult).then_inc(nmax_done, 1)

            def normalise(m):
                dve.wait_ge(p_done, 4 * (m + 1))
                link(dve.reciprocal(stat[:, 72 + 4 * m:76 + 4 * m], stat[:, 32 + 4 * m:36 + 4 * m]))
                for e in range(2):
                    for qt in range(NT):
                        o, w, i = qt * P, (qt + 1) * P, 72 + 4 * m + 2 * e + qt
                        ins = dve.tensor_scalar(pr[:, e, o:o + w], pr[:, e, o:o + w], stat[:, i:i + 1], None, ALU.mult)
                ins.then_inc(pn_done, 1)

            def gated_heads(m):
                dve.wait_ge(pv_ready, m + 1)
                dve.wait_ge(gate_done, 1 if m < 2 else 2)
                if m >= 2:
                    dve.wait_ge(oa_split, m - 1)
                dve.scalar_tensor_tensor(stg[:, m % 2, 0:S], bank[1][:, 0:S], 0.5, gm[:, m, :], ALU.mult, ALU.mult).then_inc(oa_done, 1)

            def heads_lo(m):
                dve.wait_ge(oa_hi, m + 1)
                dve.tensor_tensor(olo[:, m, :], stg[:, m % 2, 0:S], ohi[:, m, :].bitcast(F32), ALU.subtract).then_inc(oa_split, 1)

            def gate_sums(i, k0, k1):
                if i == 0 and k0 == 0:
                    dve.wait_ge(gbias_loaded, 16)
                a = accg[:, i * 512:(i + 1) * 512]
                for k in range(k0, k1):
                    if k % 4 == 0:
                        dve.wait_ge(ada_loaded[0][k // 4], 64 + 16 * (i + 1))
                    if k > 0:
                        dve.wait_ge(gate_acc, NK * i + k)
                    dve.scalar_tensor_tensor(a, ada0[:, k, :], sml[:, 24 + k:25 + k], a, ALU.mult, ALU.add).then_inc(gate_acc, 1)

            def gate_rows(i):
                dve.wait_ge(gate_ready, i + 1)
                dve.wait_ge(postw_loaded, 16)
                dve.tensor_tensor(accg[:, i * 512:(i + 1) * 512], bank[6][:, :], outb[:, 0, i * 512:(i + 1) * 512], ALU.mult).then_inc(gp_done, 1)

            def state_update(n):
                dve.wait_ge(state_ready, n + 1)
                for h in range(DH):
                    ins = dve.scalar_tensor_tensor(state[:, h, :], state[:, h, :], glx[:, n * DH + h:n * DH + h + 1], four(3)[:, h, :],
                                                   ALU.mult, ALU.add)
                ins.then_inc(state_done, 1)

            def o_sums(t):
                dve.wait_ge(osq_done, t + 1)
                dve.tensor_reduce(stat[:, 48 + 4 * t:52 + 4 * t], th[:, t, :].rearrange("p (h j) -> p h j", h=4), AX.X, ALU.add).then_inc(oss_done, 1)

            def o_scale(t):
                dve.wait_ge(orstd_done, t + 1)
                if t >= 1:
                    dve.wait_ge(oT_ready, t)
                dve.tensor_tensor(on[:, :, :], four(4 + t), over_cols(stat[:, 64 + 4 * t:68 + 4 * t]), ALU.mult).then_inc(on_done, 1)

            def o_gate(t):
                dve.wait_ge(oT_ready, t + 1)
                dve.wait_ge(oa_split, 4)
                dve.scalar_tensor_tensor(stg[:, t, :].rearrange("p (h s) -> p h s", h=4), four(4 + t), dnwh[:, :], gz[:, :, t * P:(t + 1) * P],
                                         ALU.mult, ALU.mult).then_inc(odn_done, 1)

            def dn_lo(t):
                dve.wait_ge(odn_hi, t + 1)
                dve.tensor_tensor(olo[:, 4:8, t * P:(t + 1) * P], stg[:, t, :].rearrange("p (h s) -> p h s", h=4),
                                  ohi[:, 4:8, t * P:(t + 1) * P].bitcast(F32), ALU.subtract).then_inc(odn_split, 1)

            def finish(t):
                dve.wait_ge(ysq_done, 2 * t + 2)
                dve.tensor_tensor(sml[:, 44 + t:45 + t], sml[:, 40 + 2 * t:41 + 2 * t], sml[:, 41 + 2 * t:42 + 2 * t], ALU.add).then_inc(ysum_done, 1)
                dve.wait_ge(yrstd_done, t + 1)
                dve.wait_ge(gp_done, 2)
                dve.wait_ge(xres_loaded, 16)
                for hf in range(2):
                    o = outb[:, t, hf * 512:(hf + 1) * 512]
                    link(dve.scalar_tensor_tensor(o, bank[YB[t][hf]][:, :], sml[:, 48 + t:49 + t], accg[:, hf * 512:(hf + 1) * 512],
                                                  ALU.mult, ALU.mult))
                    dve.tensor_tensor(o, o, xres[:, t, hf * 512:(hf + 1) * 512], ALU.add).then_inc(y_done, 1)

            gates_in()
            conv(0)
            gates_out()
            conv(1)
            cum_copy()
            conv_silu(0)
            conv(2)
            conv_silu(1)
            rope(0)
            conv(3)
            conv_silu(2)
            conv(4)
            conv_silu(3)
            conv(5)
            conv_silu(4)
            conv_silu(5)
            rope(1)
            columns()
            maxima(0)
            k_tokens(0)
            k_tokens(1)
            normalise(0)
            row_sum(0)
            gate(0)
            decayed(0)
            row_sum(1)
            decayed(1)
            v_tokens(0)
            v_tokens(1)
            gate_sums(0, 0, 4)
            gated_heads(0)
            first_inverse()
            maxima(1)
            rope(2)
            normalise(1)
            heads_lo(0)
            gate_sums(0, 4, 8)
            merge(1)
            gated_heads(1)
            rope(3)
            maxima(2)
            heads_lo(1)
            normalise(2)
            merge(2)
            gate_sums(1, 0, 4)
            gate(1)
            gated_heads(2)
            merge(3)
            heads_lo(2)
            maxima(3)
            gate_sums(1, 4, 8)
            normalise(3)
            merge(4)
            gate(2)
            gated_heads(3)
            heads_lo(3)
            gate_rows(0)
            merge(5)
            dve.memset(state[:, :, :], 0.0).then_inc(state_done, 1)
            gate(3)
            gate_rows(1)
            state_update(0)
            state_update(1)
            o_sums(0)
            o_scale(0)
            state_update(2)
            o_gate(0)
            dn_lo(0)
            o_sums(1)
            o_scale(1)
            o_gate(1)
            dn_lo(1)
            finish(0)
            finish(1)

        @block.tensor
        def _(pe):
            def three(out, a, b, ia, ib, start, stop, skip=False):
                pe.matmul(out, a[0][ia], b[0][ib], start=start, stop=False, skip_group_check=skip)
                pe.matmul(out, a[1][ia], b[0][ib], start=False, stop=False, skip_group_check=skip)
                return pe.matmul(out, a[0][ia], b[1][ib], start=False, stop=stop, skip_group_check=skip)

            w_parts, h_parts, o_parts = (whi, wlo), (hhi, hlo), (ohi, olo)

            pe.wait_ge(prow_loaded, 16 * 5)
            pe.wait_ge(const_loaded, 16)
            pe.transpose(bank[7][:, 0:NROWS], prow[0:NROWS, :], ident[0:NROWS, 0:NROWS]).then_inc(prow_turned, 1)
            pe.wait_ge(xn_done, NT)
            for b in range(4):
                for k in (2 * b, 2 * b + 1):
                    for t in range(NT):
                        ins = pe.transpose(bank[b][:, (k % 2) * S + t * P:(k % 2) * S + (t + 1) * P], xn[:, t, k * P:(k + 1) * P], ident)
                ins.then_inc(xT_ready, 1)

            def mod(q):
                pe.wait_ge(acc_done, q + 1)
                if q == 1:
                    pe.wait_ge(pcol_done, 1)
                if q >= 2:
                    pe.wait_ge(mod_read, q - 1)
                for i in range(4):
                    ins = pe.matmul(bank[6 + q % 2][:, i:i + 1], acc[:, q % 2, i * P:(i + 1) * P], ones[:, 0:1], start=True, stop=True)
                ins.then_inc(mod_ready, 1)

            def qkv_unit_tile(k, i):
                n, o = 2 * k + i // 6, (i % 6) * P
                return three(bank[i // 2][:, (i % 2) * S:(i % 2 + 1) * S], w_parts, h_parts,
                             (slice(None), n % SPL, slice(o, o + P)), (slice(None), k, slice(None)),
                             start=(k == 0 and i % 2 == 0), stop=(k == NK - 1), skip=True)

            def qkv_products(k):
                pe.wait_ge(hlo_done, k // 2 + 1)
                if k == 0:
                    pe.wait_ge(xT_done, 4)
                for hf in range(2):
                    pe.wait_ge(lo_done, 2 * k + hf + 1)
                    for i in range(6 * hf, 6 * hf + 6):
                        ins = qkv_unit_tile(k, i)
                    ins.then_inc(unit_done, 1)

            def last_qkv_products():
                k = NK - 1
                pe.wait_ge(lo_done, 2 * k + 2)
                for m, i in enumerate(PAIRS):
                    qkv_unit_tile(k, i)
                    qkv_unit_tile(k, i + 1).then_inc(qkv_ready, 1)

            def ba():
                pe.wait_ge(wba_loaded, 16)
                pe.wait_ge(mod_read, 3)
                for t in range(NT):
                    for k in range(NK):
                        ins = pe.matmul(bank[6][:, t * 8:t * 8 + 8], hT[:, k, t * P:(t + 1) * P], wba[:, k, :], start=(k == 0), stop=(k == NK - 1))
                ins.then_inc(ba_ready, 1)

            def half(j):
                u, n = j // 2, N1 + j
                b = bank_of_group(u)
                if j % 2 == 0:
                    if u == 0:
                        pe.wait_ge(mod_read, 4)
                    elif u == 1:
                        pe.wait_ge(conv_done, 3)
                    elif u - 2 in GQK:
                        pe.wait_ge(rope_done, ROPES.index(u - 2) + 1)
                    elif u - 2 in GV:
                        pe.wait_ge(v_copied, VS.index(u - 2) + 1)
                    else:
                        pe.wait_ge(gate_done, GATES.index(u - 2) + 1)
                pe.wait_ge(lo_done, n + 1)
                for kk in range(4):
                    k = 4 * (j % 2) + kk
                    for i in range(2):
                        out = bank[b][:, i * S:(i + 1) * S]
                        last = kk == 3 and i == 1
                        if u in GV:
                            ins = three(out, h_parts, w_parts, (slice(None), k, slice(i * P, (i + 1) * P)),
                                        (slice(None), n % SPL, slice(kk * 256, kk * 256 + 256)),
                                        start=(k == 0 and i == 0), stop=(k == NK - 1), skip=True)
                        else:
                            ins = three(out, w_parts, h_parts, (slice(None), n % SPL, slice(kk * 256 + i * P, kk * 256 + (i + 1) * P)),
                                        (slice(None), k, slice(None)), start=(k == 0 and i == 0), stop=(k == NK - 1), skip=True)
                        if last and j % 2 == 0:
                            ins.then_inc(unit_done, 1)
                        if last and j % 2 == 1:
                            ins.then_inc(group_ready, 1)

            def cum():
                g = zz[:, 0, :]
                pe.wait_ge(g_done, 1)
                for t in range(NT):
                    gt = g[:, t * DH:(t + 1) * DH]
                    pe.matmul(bank[6][:, t * DH:(t + 1) * DH], cst[:, C_TRI:C_TRI + P], gt, start=True, stop=True)
                    pe.matmul(bank[6][:, NTH + t * DH:NTH + (t + 1) * DH], cst[:, C_CHK:C_CHK + P], gt, start=True, stop=True)
                    for r in range(2):
                        o = 2 * NTH + (2 * t + r) * DH
                        ins = pe.matmul(bank[6][:, o:o + DH], cst[:, C_CHK + r * CHUNK:C_CHK + r * CHUNK + 1].to_broadcast([P, P]), gt,
                                        start=True, stop=True)
                ins.then_inc(cum_ready, 1)

            def ssq():
                pe.wait_ge(sq_done, 4)
                pe.wait_ge(cum_copied, 1)
                for a in range(2):
                    for t in range(NT):
                        for h in range(DH):
                            o = a * NTH + t * DH + h
                            ins = pe.matmul(bank[6][:, o:o + 1], sq[:, a * 4 + h, t * P:(t + 1) * P], ones[:, 0:1], start=True, stop=True)
                ins.then_inc(ssq_ready, 1)

            def k_turn():
                pe.wait_ge(silu_done, 2)
                for t in range(NT):
                    for h in range(DH):
                        ins = pe.transpose(four(2 + t)[:, h, :], qkvs[:, 4 + h, t * P:(t + 1) * P], ident)
                    ins.then_inc(ktok_ready, 1)

            def v_turn():
                pe.wait_ge(silu_done, 6)
                pe.wait_ge(row_sums, 4)
                for t in range(NT):
                    for h in range(DH):
                        ins = pe.transpose(four(4 + t)[:, h, :], qkvs[:, 8 + h, t * P:(t + 1) * P], ident)
                    ins.then_inc(vtok_ready, 1)

            def rows(t):
                pe.wait_ge(cols_done, 1)
                if t == 0:
                    pe.wait_ge(conv_done, 6)
                else:
                    pe.wait_ge(row_sums, 2)
                for b, col in ((4, 3), (5, 4)):
                    for h in range(DH):
                        i = t * DH + h
                        ins = pe.matmul(four(b)[:, h, :], cols[:, col, i:i + 1].to_broadcast([P, P]), ident, start=True, stop=True)
                ins.then_inc(rows_ready, 1)

            def kk_products(t):
                if t == 0:
                    pe.wait_ge(ktok_used, 2)
                else:
                    pe.wait_ge(a_done, 2)
                for b, o in ((2, 4), (3, 0)):
                    for h in range(DH):
                        ins = pe.matmul(four(b)[:, h, :], qkvs[:, 4 + h, t * P:(t + 1) * P], qkvs[:, o + h, t * P:(t + 1) * P],
                                        start=True, stop=True)
                ins.then_inc(kk_ready, 1)

            def z_products(l):
                for t in range(NT):
                    pe.wait_ge(ml_done, NT * l + t + 1)
                    if l == 0:
                        pe.wait_ge(a_done, 4)
                        if t == 1:
                            pe.wait_ge(vtok_used, 1)
                    else:
                        pe.wait_ge(t_done, 2 * NT + NT * (l - 2) + t + 1 if l >= 2 else 2 * t + 2)
                    for h in range(DH):
                        i = t * DH + h
                        if l == 0:
                            ins = pe.transpose(four(2 + 2 * t)[:, h, :], ml[:, i, :], ident)
                        else:
                            ins = pe.matmul(four(2 + 2 * t)[:, h, :], ml[:, i, :], tt[:, i, :], start=True, stop=True)
                    ins.then_inc(z_ready, 1)

            def x_products(l):
                for t in range(NT):
                    pe.wait_ge(z_copied, NT * (l - 1) + t + 1)
                    if l == 1 and t == 1:
                        pe.wait_ge(vtok_used, 2)
                    for h in range(DH):
                        i = t * DH + h
                        if l < LEVELS - 1:
                            pe.matmul(four(3 + 2 * t)[:, h, :], zt[:, i, :], ti[:, i, :], start=True, stop=True)
                        ins = pe.matmul(four(2 + 2 * t)[:, h, :], ti[:, i, :], zt[:, i, :], start=True, stop=True)
                    ins.then_inc(x_ready, 1)

            def w_products():
                for t in range(NT):
                    pe.wait_ge(t_done, 2 * NT + NT * (LEVELS - 2) + t + 1)
                    for h in range(DH):
                        i = t * DH + h
                        ins = pe.matmul(four(2 + 2 * t)[:, h, :], kw[:, i, :], tt[:, i, :], start=True, stop=True)
                    ins.then_inc(wT_ready, 1)

            def vnew_products(n):
                t, r = n // 2, slice((n % 2) * CHUNK, (n % 2 + 1) * CHUNK)
                pe.wait_ge(wT_copied, NT)
                pe.wait_ge(state_done, n + 1)
                if n >= 1:
                    pe.wait_ge(vnew_copied, n)
                for h in range(DH):
                    i = t * DH + h
                    pe.matmul(four(2)[r, h, :], tt[:, i, r], vb[:, i, :], start=(h == 0), stop=False, skip_group_check=True)
                    ins = pe.matmul(four(2)[r, h, :], wT[:, i, r], state[:, h, :], start=False, stop=(h == DH - 1), skip_group_check=True)
                ins.then_inc(vnew_ready, 1)
                pe.wait_ge(qd_done, t + 1)
                for h in range(DH):
                    i = t * DH + h
                    pe.matmul(four(4 + t)[r, h, :], qd[:, i, r], state[:, h, :], start=(h == 0), stop=False, skip_group_check=True)

            def state_products(n):
                t, r = n // 2, slice((n % 2) * CHUNK, (n % 2 + 1) * CHUNK)
                pe.wait_ge(vnew_copied, n + 1)
                if n < NCH - 1:
                    for h in range(DH):
                        i = t * DH + h
                        ins = pe.matmul(four(3)[:, h, :], kd[r, i, :], vnew[r, i, :], start=True, stop=True)
                    ins.then_inc(state_ready, 1)
                if n % 2 == 1:
                    for h in range(DH):
                        i = t * DH + h
                        ins = pe.matmul(four(4 + t)[:, h, :], qkd[:, i, :], vnew[:, i, :], start=False, stop=True, skip_group_check=True)
                    ins.then_inc(o_ready, 1)

            def o_turn(t):
                pe.wait_ge(on_done, t + 1)
                for h in range(DH):
                    ins = pe.transpose(four(4 + t)[:, h, :], on[:, h, :], ident)
                ins.then_inc(oT_ready, 1)

            def scores(m):
                if m < 2:
                    pe.wait_ge(rope_done, 2)
                else:
                    pe.wait_ge(rope_done, 4)
                if m == 0:
                    pe.wait_ge(conv_done, 4)
                    pe.wait_ge(lsq_done, 2)
                else:
                    pe.wait_ge(oa_done, m)
                for qt in range(NT):
                    o, w = qt * P, (qt + 1) * P
                    for e in range(2):
                        r = slice(e * AD, (e + 1) * AD)
                        ins = pe.matmul(bank[ATT[e]][:, o:o + w], qT[r, m, o:o + P], kT[r, m, 0:w], start=True, stop=True)
                ins.then_inc(s_ready, 1)

            def p_turn(m):
                pe.wait_ge(pn_done, m + 1)
                for e in range(2):
                    for i in range(3):
                        ins = pe.transpose(bank[ATT[e]][:, i * P:(i + 1) * P], pr[:, e, i * P:(i + 1) * P], ident)
                ins.then_inc(pT_ready, 1)

            def pv(m):
                pe.wait_ge(v_copied, 1 if m < 2 else 2)
                pe.wait_ge(pT_copied, 2 * m + 2)
                for e in range(2):
                    r, cols_ = slice(e * AD, (e + 1) * AD), slice((2 * m + e) * AD, (2 * m + e + 1) * AD)
                    pe.matmul(bank[1][r, 0:S], vt[:, 0, cols_], pT[:, e, 0:S], start=True, stop=False, skip_group_check=True)
                    ins = pe.matmul(bank[1][r, P:S], vt[:, 1, cols_], pT[:, e, S:S + P], start=False, stop=True, skip_group_check=True)
                ins.then_inc(pv_ready, 1)

            def gate_sum(i):
                pe.wait_ge(gate_acc, NK * (i + 1))
                if i == 0:
                    pe.wait_ge(pT_copied, 8)
                else:
                    pe.wait_ge(gp_done, 1)
                pe.matmul(bank[6][:, :], ones[:, :], accg[:, i * 512:(i + 1) * 512], start=True, stop=True).then_inc(gate_ready, 1)

            def y_products(k, t):
                n = N1 + N2 + k
                pe.wait_ge(lo_done, n + 1)
                if k < 4:
                    pe.wait_ge(oa_split, k + 1)
                else:
                    pe.wait_ge(odn_split, t + 1)
                if k == 0:
                    if t == 0:
                        pe.wait_ge(gate_done, 4)
                    else:
                        pe.wait_ge(oa_done, 4)
                        pe.wait_ge(gp_done, 2)
                for hf in range(2):
                    ins = three(bank[YB[t][hf]][:, :], o_parts, w_parts, (slice(None), k, slice(t * P, (t + 1) * P)),
                                (slice(None), n % SPL, slice(hf * 512, (hf + 1) * 512)), start=(k == 0), stop=(k == NK - 1))
                if k == NK - 1:
                    ins.then_inc(y_ready, 1)
                elif t == NT - 1:
                    ins.then_inc(unit_done, 1)

            mod(0)
            mod(1)
            qkv_products(0)
            qkv_products(1)
            mod(2)
            qkv_products(2)
            qkv_products(3)
            mod(3)
            for k in range(4, NK - 1):
                qkv_products(k)
            last_qkv_products()
            ba()
            half(0)
            cum()
            half(1)
            half(2)
            half(3)
            half(4)
            k_turn()
            ssq()
            half(5)
            scores(0)
            half(6)
            rows(0)
            p_turn(0)
            half(7)
            kk_products(0)
            rows(1)
            half(8)
            kk_products(1)
            v_turn()
            pv(0)
            half(9)
            z_products(0)
            scores(1)
            half(10)
            z_products(1)
            p_turn(1)
            half(11)
            x_products(1)
            pv(1)
            half(12)
            z_products(2)
            scores(2)
            half(13)
            x_products(2)
            p_turn(2)
            half(14)
            z_products(3)
            pv(2)
            half(15)
            x_products(3)
            half(16)
            z_products(4)
            scores(3)
            half(17)
            x_products(4)
            p_turn(3)
            half(18)
            z_products(5)
            pv(3)
            gate_sum(0)
            half(19)
            x_products(5)
            gate_sum(1)
            y_products(0, 0)
            w_products()
            y_products(0, 1)
            vnew_products(0)
            y_products(1, 0)
            state_products(0)
            y_products(1, 1)
            vnew_products(1)
            y_products(2, 0)
            state_products(1)
            y_products(2, 1)
            vnew_products(2)
            y_products(3, 0)
            state_products(2)
            y_products(3, 1)
            vnew_products(3)
            o_turn(0)
            for k in range(4, NK):
                y_products(k, 0)
                if k == 4:
                    state_products(3)
            o_turn(1)
            for k in range(4, NK):
                y_products(k, 1)

    return nc


def constants():
    f = np.float32
    c = np.zeros((P, NCONST), f)
    rope = AD // 4
    half = rope // 2
    inv = np.power(f(500000.0), -np.arange(0, rope, 2, dtype=f) / f(rope)).astype(f)
    ang = (np.arange(S, dtype=f)[None, :] * inv[:, None]).astype(f)
    c[:, C_COS:C_COS + S] = 1.0
    for p in range(P):
        d = p % AD
        if d < rope:
            c[p, C_COS:C_COS + S] = np.cos(ang[d % half])
            c[p, C_SIN:C_SIN + S] = (-1.0 if d < half else 1.0) * np.sin(ang[d % half])
    i, j = np.arange(P)[:, None], np.arange(P)[None, :]
    same = i // CHUNK == j // CHUNK
    c[:, C_ID:C_ID + P] = i == j
    c[:, C_TRI:C_TRI + P] = same & (i <= j)
    c[:, C_CHK:C_CHK + P] = same
    c[:, C_MA:C_MA + P] = np.where(same & (i > j), 1e30, -1e30)
    c[:, C_MQ:C_MQ + P] = np.where(same & (i <= j), 1e30, -1e30)
    c[:, C_CM + P:C_CM + 2 * P] = np.where(j <= i, 0.0, -1e30)
    for l in range(LEVELS):
        b = 1 << l
        c[:, C_LV + l * P:C_LV + (l + 1) * P] = (i // (2 * b) == j // (2 * b)) & (i // b % 2 == 1) & (j // b % 2 == 0)
    return c


_INS = ["x", "c", "ada_w", "ada_b", "pre_norm_w", "post_norm_w", "w_in", "conv_w", "a_log", "dt_bias", "dn_norm_w", "w_out"]


def kernel(**inputs):
    import concourse.bacc as bacc
    from concourse.bass_utils import run_bass_kernel_spmd

    nc = bacc.Bacc("TRN2", target_bir_lowering=False, num_devices=1)
    arrays, aps = {}, {}
    for name in _INS + ["consts"]:
        a = constants() if name == "consts" else np.ascontiguousarray(inputs[name])
        arrays[f"in_{name}"] = a
        aps[name] = nc.dram_tensor(f"in_{name}", a.shape, mybir.dt.from_np(a.dtype), kind="ExternalInput").ap()
    out = nc.dram_tensor("out_y", (1, S, D), F32, kind="ExternalOutput").ap()
    build(nc, aps["x"], aps["c"], aps["ada_w"], aps["ada_b"], aps["pre_norm_w"], aps["post_norm_w"], aps["w_in"], aps["conv_w"],
          aps["a_log"], aps["dt_bias"], aps["dn_norm_w"], aps["w_out"], aps["consts"], out)
    r = run_bass_kernel_spmd(nc, [arrays], core_ids=[0])
    return r.results[0]["out_y"]
```

```python
from contextlib import ExitStack

import numpy as np

import concourse.bass as bass
from concourse import mybir

F32 = mybir.dt.float32
F32R = mybir.dt.float32r
ACT = mybir.ActivationFunctionType
ALU = mybir.AluOpType
AX = mybir.AxisListType

P = 128
D = 1024
S = 256
NT = S // P
NK = D // P
AH, AD = 8, 64
AW = AH * AD
DH, DK = 4, 128
DW = DH * DK
CHUNK = 64
NCH = S // CHUNK
EPS = 1e-6
NTH = NT * DH

MQ, MK, MV, MG = 0, AW, 2 * AW, 3 * AW
DQ, DZ, DBA = 4 * AW, 4 * AW + 3 * DW, 4 * AW + 4 * DW
NQKV = 3 * DW // P

R_C, R_SHIFT, R_SCALE, R_PRE, R_DNW, R_CONV = 0, 8, 16, 24, 32, 33
NROWS = R_CONV + 4 * NQKV

LEVELS = 6
HALF = P // 2
C_ID, C_COS, C_SIN, C_TRI, C_CHK, C_MA, C_MQ, C_CM, C_LV = 0, 128, 384, 640, 768, 896, 1024, 1152, 1408
NCONST = C_LV + LEVELS * HALF

UNIT = 1024
RAW = 5
SPL = 4
N1 = 2 * NK
N2 = 20
N3 = NK
HQ = 3 * DW // 2
GROUPS = [MQ, MK, MG, MV, MQ + 256, MK + 256, MV + 256, MG + 256, DZ, DZ + 256]


def build(nc, x, c, ada_w, ada_b, pre_w, post_w, w_in, conv_w, a_log, dt_bias, dnw, w_out, const, out):
    with ExitStack() as ctx:
        def sb(name, shape, dt=F32, into=ctx):
            return into.enter_context(nc.sbuf_tensor(name, shape, dt))

        def sem(name):
            return ctx.enter_context(nc.semaphore(name))

        bank = [ctx.enter_context(nc.psum_tensor(f"bank{b}", [P, 512], F32)) for b in range(8)]

        cst = sb("cst", [P, NCONST])
        ident = cst[:, C_ID:C_ID + P]
        pcol = sb("pcol", [P, NROWS])
        convh = sb("convh", [P, 4 * NQKV])
        dnwh = sb("dnwh", [P, 1])
        ones = sb("ones", [P, P])
        epsc = sb("epsc", [P, 2])
        sml = sb("sml", [P, 64])
        dab = sb("dab", [P, 8])
        mod_a = sb("mod_a", [P, NK])
        mod_b = sb("mod_b", [P, NK])
        zz = sb("zz", [P, 6, NTH])
        ssq = sb("ssq", [P, 2, NTH])
        lsq = sb("lsq", [P, 2, NTH])
        gcs = sb("gcs", [P, 4 * NTH])
        cols = sb("cols", [P, 8, NTH])
        ecol = sb("ecol", [P, 3, NTH])
        glx = sb("glx", [P, NCH * DH])
        stat = sb("stat", [P, 96])
        wba = sb("wba", [P, NK, 8])
        hhi = sb("hhi", [P, NK, S], F32R)
        hlo = sb("hlo", [P, NK, S], F32R)
        raw = sb("raw", [P, RAW, UNIT])
        whi = sb("whi", [P, SPL, UNIT], F32R)
        wlo = sb("wlo", [P, SPL, UNIT], F32R)
        accg = sb("accg", [P, D])
        th = sb("th", [P, 2, 512])
        prow = th[:, 0, 0:P]
        qT = sb("qT", [P, 4, S])
        kT = sb("kT", [P, 4, S])
        vt = sb("vt", [P, NT, AW])
        gm = sb("gm", [P, 4, S])
        gz = sb("gz", [P, 4, S])
        stg = sb("stg", [P, 2, 512])

        with ExitStack() as e:
            ada0 = sb("ada0", [P, NK, 512], into=e)
        with ExitStack() as e:
            xres = sb("xres", [P, NT, D], into=e)
            outb = sb("outb", [P, NT, D], into=e)
        sb("hold_ada0", [P, NK * 512])
        with ExitStack() as e:
            qkvs = sb("qkvs", [P, NQKV, S], into=e)
            acc = sb("acc", [P, 2, 512], into=e)
        with ExitStack() as e:
            ohi = sb("ohi", [P, NK, S], F32R, into=e)
            olo = sb("olo", [P, NK, S], F32R, into=e)
        sb("hold_qkvs", [P, NQKV * S + 1024])
        rot = sb("rot", [P, 3, 512])
        acc_p = rot
        pr, pT = sb("pr", [P, 2, 384]), sb("pT", [P, 2, 384])
        with ExitStack() as e:
            xs = sb("xs", [P, NT, D], into=e)
            xT = xs[:, :, :].rearrange("p t (k s) -> p (t k) s", s=S)
            xn = sb("xn", [P, NT, D], into=e)
            ada1 = sb("ada1", [P, NK, 512], into=e)
            hT = sb("hT", [P, NK, S], into=e)
            cv = sb("cv", [P, NQKV, S], into=e)
        def th_array(name):
            return sb(name, [P, NTH, P])
        kw, kd, vb = th_array("kw"), th_array("kd"), th_array("vb")
        dec = sb("dec", [P, 2, NTH, P])
        am, qkd, qd = th_array("am"), th_array("qkd"), th_array("qd")
        ti, tt = th_array("ti"), th_array("tt")
        zt = sb("zt", [P, NTH, HALF])
        wT, vnew = am, kw
        state = sb("state", [P, 2, DH, P])
        on = sb("on", [P, DH, P])
        ada = [ada0, ada1]
        sq = dec[:, :, :, :].rearrange("p a b c -> p (a b c)").rearrange("p (j n) -> p j n", n=512)

        prow_loaded, ident_loaded, const_loaded, dab_loaded, wba_loaded = map(
            sem, ("prow_loaded", "ident_loaded", "const_loaded", "dab_loaded", "wba_loaded"))
        gbias_loaded, postw_loaded, xres_loaded, stored = map(sem, ("gbias_loaded", "postw_loaded", "xres_loaded", "stored"))
        x_loaded = [sem(f"x_loaded{t}") for t in range(NT)]
        ada_loaded = [[sem(f"ada_loaded{s}{h}") for h in range(2)] for s in range(2)]
        raw_loaded = [sem(f"raw_loaded{s}") for s in range(RAW)]
        dve_step, act_step = sem("dve_step"), sem("act_step")
        pool_init, tt_init, dve_init, prow_turned, pcol_done, c_tanh, sc_done, xms_done, xstd_done, xrstd_done, xn_done, xT_ready, xT_done, expa_done = map(
            sem, ("pool_init", "tt_init", "dve_init", "prow_turned", "pcol_done", "c_tanh", "sc_done", "xms_done", "xstd_done",
                  "xrstd_done", "xn_done", "xT_ready",
                  "xT_done", "expa_done"))
        acc_done, pool_acc_done, mod_ready, mod_read, h_done, hhi_done, hlo_done = map(
            sem, ("acc_done", "pool_acc_done", "mod_ready", "mod_read", "h_done", "hhi_done", "hlo_done"))
        hi_done, lo_done, dve_lo_done, unit_done, group_ready = map(sem, ("hi_done", "lo_done", "dve_lo_done", "unit_done", "group_ready"))
        qkv_ready, tap_done, conv_done, ctanh_done, silu_done, sq_done = map(
            sem, ("qkv_ready", "tap_done", "conv_done", "ctanh_done", "silu_done", "sq_done"))
        ba_ready, ba_abs, ba_ln, g_done, cum_ready, cum_copied, qtok_ready, sq_summed, lsq_done, cols_done, ecol_done = map(
            sem, ("ba_ready", "ba_abs", "ba_ln", "g_done", "cum_ready", "cum_copied", "qtok_ready", "sq_summed", "lsq_done", "cols_done",
                  "ecol_done"))
        rows_ready, rows_exp, row_sums, dec_done, kk_ready, a_done, ktok_ready, ktok_used, vtok_ready, vtok_used, qd_done = map(
            sem, ("rows_ready", "rows_exp", "row_sums", "dec_done", "kk_ready", "a_done", "ktok_ready", "ktok_used",
                  "vtok_ready", "vtok_used", "qd_done"))
        z_ready, z_masked, turned, ti_done, x_ready, t_done, wT_ready, wT_copied = map(
            sem, ("z_ready", "z_masked", "turned", "ti_done", "x_ready", "t_done", "wT_ready", "wT_copied"))
        vnew_ready, vnew_copied, state_ready, state_done, o_ready, osq_done, oss_done, ostd_done, on_done = map(
            sem, ("vnew_ready", "vnew_copied", "state_ready", "state_done", "o_ready", "osq_done", "oss_done", "ostd_done",
                  "on_done"))
        oT_ready, odn_done, odn_hi, odn_split = map(sem, ("oT_ready", "odn_done", "odn_hi", "odn_split"))
        shuffled, times_sin, rope_done, v_copied, gtanh_done, gate_done = map(
            sem, ("shuffled", "times_sin", "rope_done", "v_copied", "gtanh_done", "gate_done"))
        s_ready, nmax_done, p_done, pn_done, pT_ready, pT_copied, pv_ready, oa_done, oa_hi, oa_split = map(
            sem, ("s_ready", "nmax_done", "p_done", "pn_done", "pT_ready", "pT_copied", "pv_ready", "oa_done", "oa_hi",
                  "oa_split"))
        gate_acc, gate_ready, gp_done, y_ready, ysq_done, ysum_done, ygate_done, ystd_done, y_done = map(
            sem, ("gate_acc", "gate_ready", "gp_done", "y_ready", "ysq_done", "ysum_done", "ygate_done", "ystd_done", "y_done"))

        def raw_u(n):
            return raw[:, n % RAW, 0:(HQ if n < N1 else UNIT)]

        def split_u(buf, n):
            return buf[:, n % SPL, 0:(HQ if n < N1 else UNIT)]

        def four(b):
            return bank[b][:, :].rearrange("p (h j) -> p h j", h=4)

        def two(b):
            return bank[b][:, :].rearrange("p (a s) -> p a s", a=2)

        def heads(a, t):
            return a[:, t * DH:(t + 1) * DH, :]

        def odd(ap, l):
            return ap.rearrange("p (n two b) -> p n two b", two=2, b=1 << l)[:, :, 1, :]

        def heads_odd(a, t, l):
            return heads(a, t).rearrange("p h (n two b) -> p (h n) two b", two=2, b=1 << l)[:, :, 1, :]

        def halves(b, o):
            return bank[b][:, o:o + DH * HALF].rearrange("p (h j) -> p h j", h=DH)

        def over_cols(ap):
            return ap.unsqueeze(2).to_broadcast([P, DH, P])

        BULK, ATT, YB = [7, 0], [1, 6], [[7, 0], [1, 6]]
        GQK = {0: (qT, 0), 1: (kT, 0), 4: (qT, 2), 5: (kT, 2)}
        GV = {3: 0, 6: 1}
        GG = {2: (gm, 0), 7: (gm, 2), 8: (gz, 0), 9: (gz, 2)}
        ROPES, VS, GATES = sorted(GQK), sorted(GV), sorted(GG)
        QKV_ORDER = [4, 5, 6, 7, 0, 1, 2, 3, 8, 9, 10, 11]
        PAIRS = QKV_ORDER[::2]

        def bank_of_group(u):
            return BULK[u % 2]

        def low_part(n):
            if n % 3 == 1:
                return dve_lo_done, n // 3 + 1
            return lo_done, n + 1 - (n + 1) // 3

        def used_up(n):
            if n < N1 - 2:
                return unit_done, n + 1
            if n < N1:
                return qkv_ready, len(PAIRS)
            j = n - N1
            if j < N2:
                return (unit_done, N1 - 2 + j // 2 + 1) if j % 2 == 0 else (group_ready, j // 2 + 1)
            return unit_done, N1 - 2 + N2 // 2 + j - N2 + 1

        block = ctx.enter_context(nc.Block())

        @block.sync
        def _(sp):
            for r0, n, src in ((R_C, 8, c.rearrange("a (r p) -> (a r) p", p=P)),
                               (R_SHIFT, 16, ada_b[:, 0:2 * D].rearrange("a (r p) -> (a r) p", p=P)),
                               (R_PRE, 8, pre_w.rearrange("a (r p) -> (a r) p", p=P)),
                               (R_DNW, 1, dnw),
                               (R_CONV, 4 * NQKV, conv_w.rearrange("a j (i p) -> (a j i) p", p=P))):
                sp.dma_start(prow[r0:r0 + n, :], src).then_inc(prow_loaded, 16)
            sp.dma_start(ident, const[:, C_ID:C_ID + P]).then_inc(ident_loaded, 16)

            def load_ada(q):
                if q >= 2:
                    sp.wait_ge(acc_done, q - 1)
                for hf in range(2):
                    for part in range(2):
                        src = ada_w[0, 4 * hf * P:(4 * hf + 4) * P, part * D + q * 256:part * D + (q + 1) * 256]
                        sp.dma_start(ada[q % 2][:, 4 * hf:4 * hf + 4, part * 256:(part + 1) * 256],
                                     src.rearrange("(k p) n -> p k n", p=P)).then_inc(ada_loaded[q % 2][hf], 16)

            def load_unit(n):
                if n >= RAW:
                    sp.wait_ge(*low_part(n - RAW))
                if n < N1:
                    k, hf = n // 2, n % 2
                    src, dst = w_in[0, k * P:(k + 1) * P, DQ + hf * HQ:DQ + (hf + 1) * HQ], raw_u(n)
                elif n < N1 + N2:
                    u, hf = (n - N1) // 2, (n - N1) % 2
                    src = w_in[0, hf * 4 * P:(hf + 1) * 4 * P, GROUPS[u]:GROUPS[u] + 256].rearrange("(k p) n -> p k n", p=P)
                    dst = raw_u(n).rearrange("p (k n) -> p k n", k=4)
                else:
                    k = n - N1 - N2
                    src, dst = w_out[0, k * P:(k + 1) * P, :], raw_u(n)
                sp.dma_start(dst, src).then_inc(raw_loaded[n % RAW], 16)

            def load_gate(i):
                if i == 0:
                    sp.wait_ge(acc_done, 3)
                else:
                    sp.wait_ge(gate_acc, NK)
                for hf in range(2):
                    src = ada_w[0, 4 * hf * P:(4 * hf + 4) * P, 2 * D + i * 512:2 * D + (i + 1) * 512]
                    sp.dma_start(ada0[:, 4 * hf:4 * hf + 4, :],
                                 src.rearrange("(k p) n -> p k n", p=P)).then_inc(ada_loaded[0][hf], 16)

            def load_x(t):
                sp.dma_start(xs[:, t, :], x[0, t * P:(t + 1) * P, :]).then_inc(x_loaded[t], 16)

            def load_constants():
                sp.dma_start(cst[:, C_COS:], const[:, C_COS:]).then_inc(const_loaded, 16)

            def load_gates():
                sp.dma_start(dab[:, 0:4], dt_bias[0].partition_broadcast(P)).then_inc(dab_loaded, 16)
                sp.dma_start(dab[:, 4:8], a_log[0].partition_broadcast(P)).then_inc(dab_loaded, 16)
                sp.dma_start(wba[:, :, :], w_in[0, :, DBA:DBA + 8].rearrange("(k p) n -> p k n", p=P)).then_inc(wba_loaded, 16)

            def load_gate_bias():
                sp.wait_ge(pool_init, 1)
                sp.dma_start(accg[0:1, :], ada_b[:, 2 * D:3 * D]).then_inc(gbias_loaded, 16)

            def load_last():
                sp.wait_ge(gate_acc, 2 * NK)
                sp.dma_start(outb[:, 0, :], post_w[0].partition_broadcast(P)).then_inc(postw_loaded, 16)
                sp.dma_start(xres[:, :, :], x[0].rearrange("(t p) n -> p t n", p=P)).then_inc(xres_loaded, 16)

            load_x(0)
            load_gate_bias()
            load_x(1)
            load_ada(0)
            load_unit(1)
            load_unit(2)
            load_unit(0)
            load_unit(3)
            load_ada(1)
            load_unit(4)
            load_unit(5)
            load_unit(6)
            load_ada(2)
            load_unit(7)
            load_unit(8)
            load_unit(9)
            load_ada(3)
            load_unit(10)
            load_gates()
            load_unit(11)
            load_unit(12)
            load_unit(13)
            load_unit(14)
            load_unit(15)
            load_unit(16)
            load_unit(17)
            load_unit(18)
            load_constants()
            load_unit(19)
            load_unit(20)
            load_unit(21)
            load_unit(22)
            load_unit(23)
            load_unit(24)
            load_unit(25)
            load_unit(26)
            load_unit(27)
            load_gate(0)
            load_unit(28)
            load_unit(29)
            load_unit(30)
            load_unit(31)
            load_unit(32)
            load_unit(33)
            load_unit(34)
            load_gate(1)
            load_unit(35)
            load_unit(36)
            load_unit(37)
            load_unit(38)
            load_unit(39)
            load_unit(40)
            load_unit(41)
            load_last()
            load_unit(42)
            load_unit(43)

            for t in range(NT):
                for hf in range(2):
                    sp.wait_ge(y_done, 2 * t + hf + 1)
                    sp.dma_start(out[0, t * P:(t + 1) * P, hf * 512:(hf + 1) * 512],
                                 outb[:, t, hf * 512:(hf + 1) * 512]).then_inc(stored, 16)
            sp.wait_ge(stored, 16 * 2 * NT)

        @block.gpsimd
        def _(pool):
            pool.memset(accg[:, :], 0.0).then_inc(pool_init, 1)

            def lo(n):
                pool.wait_ge(hi_done, n + 1)
                pool.tensor_tensor(split_u(wlo, n), raw_u(n), split_u(whi, n).bitcast(F32), ALU.subtract).then_inc(lo_done, 1)

            def first_mod_sum(q):
                pool.wait_ge(sc_done, 1)
                pool.wait_ge(ada_loaded[q % 2][0], 32 * (q // 2 + 1))
                if q >= 2:
                    pool.wait_ge(acc_done, q - 1)
                pool.tensor_scalar(acc_p[:, q % 2, :], ada[q % 2][:, 0, :], sml[:, 24:25], None, ALU.mult).then_inc(pool_acc_done, 1)

            def start_inverse():
                pool.wait_ge(ba_ready, 1)
                pool.wait_ge(hlo_done, 4)
                pool.wait_ge(hhi_done, 4)
                pool.tensor_copy(tt[:, :, :], ident.unsqueeze(1).to_broadcast([P, NTH, P])).then_inc(tt_init, 1)

            def rope_sin(r):
                pool.wait_ge(const_loaded, 16)
                pool.wait_ge(shuffled, r + 1)
                if r >= 1:
                    pool.wait_ge(rope_done, r)
                pool.tensor_tensor(rot[:, 1, :].rearrange("p (a s) -> p a s", a=2), rot[:, 0, :].rearrange("p (a s) -> p a s", a=2),
                                   cst[:, C_SIN:C_SIN + S].unsqueeze(1).to_broadcast([P, 2, S]), ALU.mult).then_inc(times_sin, 1)

            first_mod_sum(0)
            lo(0)
            first_mod_sum(1)
            lo(2)
            lo(3)
            first_mod_sum(2)
            lo(5)
            lo(6)
            lo(8)
            first_mod_sum(3)
            lo(9)
            lo(11)
            lo(12)
            lo(14)
            lo(15)
            lo(17)
            lo(18)
            lo(20)
            rope_sin(0)
            rope_sin(1)
            lo(21)
            lo(23)
            lo(24)
            lo(26)
            start_inverse()
            lo(27)
            rope_sin(2)
            rope_sin(3)
            lo(29)
            lo(30)
            lo(32)
            lo(33)
            lo(35)
            lo(36)
            lo(38)
            lo(39)
            lo(41)
            lo(42)

        @block.scalar
        def _(act):
            steps = [0]

            def link(ins):
                steps[0] += 1
                ins.then_inc(act_step, 1)
                act.wait_ge(act_step, steps[0])

            def hi(n):
                act.wait_ge(raw_loaded[n % RAW], 16 * (n // RAW + 1))
                if n >= SPL:
                    act.wait_ge(*used_up(n - SPL))
                act.activation(split_u(whi, n), raw_u(n), ACT.Copy).then_inc(hi_done, 1)

            act.wait_ge(pcol_done, 1)
            act.activation(sml[:, 0:8], pcol[:, R_C:R_C + 8], ACT.Tanh, scale=0.5).then_inc(c_tanh, 1)
            for t in range(NT):
                act.wait_ge(x_loaded[t], 16)
                act.activation(xn[:, t, :], xs[:, t, :], ACT.Square, accum_out=sml[:, 16 + t:17 + t]).then_inc(xms_done, 1)
            act.wait_ge(xms_done, 2)
            act.wait_ge(dve_init, 1)
            act.activation(sml[:, 18:20], sml[:, 16:18], ACT.Sqrt, scale=1.0 / D, bias=epsc[:, 0:1]).then_inc(xstd_done, 1)
            act.wait_ge(xrstd_done, 1)
            for t in range(NT):
                act.activation(xn[:, t, :], xs[:, t, :], ACT.Copy, scale=sml[:, 20 + t:21 + t]).then_inc(xn_done, 1)

            def xT_copy(b):
                act.wait_ge(xT_ready, b + 1)
                act.activation(xT[:, 2 * b:2 * b + 2, :], two(b), ACT.Copy).then_inc(xT_done, 1)

            def h_hi(q):
                act.wait_ge(h_done, q + 1)
                act.activation(hhi[:, 2 * q:2 * q + 2, :], hT[:, 2 * q:2 * q + 2, :], ACT.Copy).then_inc(hhi_done, 1)

            def taps(m):
                act.wait_ge(qkv_ready, m + 1)
                for i in (PAIRS[m], PAIRS[m] + 1):
                    act.activation(cv[:, i, :], bank[i // 2][:, (i % 2) * S:(i % 2 + 1) * S], ACT.Copy,
                                   scale=convh[:, 3 * NQKV + i:3 * NQKV + i + 1]).then_inc(tap_done, 1)

            def conv_tanh(m):
                i = PAIRS[m]
                act.wait_ge(conv_done, m + 1)
                if m >= 2:
                    act.wait_ge(silu_done, m - 1)
                act.activation(th[:, m % 2, :].rearrange("p (a s) -> p a s", a=2), cv[:, i:i + 2, :], ACT.Tanh).then_inc(ctanh_done, 1)

            def squares(j):
                act.wait_ge((ktok_ready, qtok_ready)[j // 2], j % 2 + 1)
                act.activation(sq[:, j, :], bank[(2, 3, 6, 1)[j]][:, :], ACT.Square).then_inc(sq_done, 1)

            def softplus():
                act.wait_ge(ba_abs, 1)
                link(act.activation(zz[:, 2:4, :], zz[:, 4:6, :], ACT.Exp, scale=-1.0))
                act.activation(zz[:, 4:6, :], zz[:, 2:4, :], ACT.Ln, bias=1.0).then_inc(ba_ln, 1)
                act.wait_ge(dab_loaded, 32)
                act.activation(dab[:, 4:8], dab[:, 4:8], ACT.Exp).then_inc(expa_done, 1)

            def norms():
                act.wait_ge(sq_summed, 4)
                act.activation(lsq[:, 0, :], ssq[:, 0, :], ACT.Ln, bias=epsc[:, 0:1]).then_inc(lsq_done, 1)
                act.activation(lsq[:, 1, :], ssq[:, 1, :], ACT.Ln, bias=epsc[:, 1:2], scale=float(DK)).then_inc(lsq_done, 1)

            def factors():
                act.wait_ge(cols_done, 1)
                act.activation(ecol[:, :, :], cols[:, 0:3, :], ACT.Exp).then_inc(ecol_done, 1)
                act.activation(glx[:, :], gcs[:, 2 * NTH:], ACT.Exp).then_inc(ecol_done, 1)

            def decays(t):
                act.wait_ge(rows_ready, t + 1)
                act.activation(heads(qd, t), four(5), ACT.Exp).then_inc(rows_exp, 1)
                for a in range(2):
                    act.wait_ge(row_sums, 2 * t + a + 1)
                    act.activation(heads(dec[:, a, :, :], t), heads(dec[:, a, :, :], t), ACT.Exp).then_inc(dec_done, 1)

            def ti_copy(l, t):
                act.wait_ge(turned, NT * (l - 1) + t + 1)
                act.activation(heads(ti, t), four(3 + 2 * t), ACT.Copy).then_inc(ti_done, 1)

            def v_copy(i):
                u = VS[i]
                act.wait_ge(group_ready, u + 1)
                act.activation(vt[:, :, i * 256:(i + 1) * 256], two(bank_of_group(u)), ACT.Copy).then_inc(v_copied, 1)

            def gate_tanh(i):
                u = GATES[i]
                act.wait_ge(group_ready, u + 1)
                act.wait_ge(silu_done, 6)
                if i >= 2:
                    act.wait_ge(gate_done, i - 1)
                act.activation(th[:, i % 2, :], bank[bank_of_group(u)][:, :], ACT.Tanh, scale=0.5).then_inc(gtanh_done, 1)

            def probs(m):
                act.wait_ge(nmax_done, m + 1)
                if m >= 1:
                    act.wait_ge(pT_ready, m)
                for e in range(2):
                    for qt in range(NT):
                        i, o, w = 2 * (2 * m + e) + qt, qt * P, (qt + 1) * P
                        act.activation(pr[:, e, o:o + w], bank[ATT[e]][:, o:o + w], ACT.Exp, scale=AD ** -0.5,
                                       bias=stat[:, 16 + i:17 + i], accum_out=stat[:, 32 + i:33 + i]).then_inc(p_done, 1)

            def pT_copy(m):
                act.wait_ge(pT_ready, m + 1)
                if m >= 1:
                    act.wait_ge(pv_ready, m)
                for e in range(2):
                    act.activation(pT[:, e, :], bank[ATT[e]][:, 0:384], ACT.Copy).then_inc(pT_copied, 1)

            def heads_hi(m):
                if m == 0:
                    act.wait_ge(kk_ready, 2)
                    act.wait_ge(vtok_ready, 2)
                    act.wait_ge(qd_done, 2)
                act.wait_ge(oa_done, m + 1)
                act.activation(ohi[:, m, :], stg[:, m % 2, 0:S], ACT.Copy).then_inc(oa_hi, 1)

            def wT_copy(t):
                act.wait_ge(wT_ready, t + 1)
                act.activation(heads(wT, t), four(2 + 2 * t), ACT.Copy, scale=-1.0).then_inc(wT_copied, 1)

            def vnew_copy(n):
                act.wait_ge(vnew_ready, n + 1)
                r = slice((n % 2) * CHUNK, (n % 2 + 1) * CHUNK)
                act.activation(heads(vnew, n // 2)[r], four(2)[r], ACT.Copy).then_inc(vnew_copied, 1)

            def o_norm(t):
                act.wait_ge(o_ready, t + 1)
                act.wait_ge(gate_done, 4)
                act.activation(th[:, t, :], bank[4 + t][:, :], ACT.Square).then_inc(osq_done, 1)
                act.wait_ge(oss_done, t + 1)
                act.activation(stat[:, 56 + 4 * t:60 + 4 * t], stat[:, 48 + 4 * t:52 + 4 * t], ACT.Sqrt, scale=1.0 / DK,
                               bias=epsc[:, 0:1]).then_inc(ostd_done, 1)

            def dn_hi(t):
                act.wait_ge(odn_done, t + 1)
                act.activation(ohi[:, 4:8, t * P:(t + 1) * P], stg[:, t, :].rearrange("p (h s) -> p h s", h=4), ACT.Copy).then_inc(odn_hi, 1)

            def y_norm(t):
                act.wait_ge(oss_done, 2)
                for hf in range(2):
                    act.wait_ge(y_ready, 1 if t == 0 else 2 + hf)
                    if t >= 1 and hf == 0:
                        act.wait_ge(ysq_done, 2 * t)
                    act.activation(th[:, hf, :], bank[YB[t][hf]][:, :], ACT.Square,
                                   accum_out=sml[:, 40 + 2 * t + hf:41 + 2 * t + hf]).then_inc(ysq_done, 1)
                act.wait_ge(ysum_done, t + 1)
                act.activation(sml[:, 46 + t:47 + t], sml[:, 44 + t:45 + t], ACT.Sqrt, scale=1.0 / D, bias=epsc[:, 0:1]).then_inc(ystd_done, 1)

            xT_copy(0)
            hi(0)
            hi(1)
            hi(2)
            hi(3)
            h_hi(0)
            xT_copy(1)
            xT_copy(2)
            xT_copy(3)
            hi(4)
            hi(5)
            h_hi(1)
            hi(6)
            hi(7)
            hi(8)
            hi(9)
            h_hi(2)
            hi(10)
            hi(11)
            hi(12)
            h_hi(3)
            hi(13)
            hi(14)
            hi(15)
            hi(16)
            taps(0)
            taps(1)
            conv_tanh(0)
            taps(2)
            hi(17)
            conv_tanh(1)
            hi(18)
            taps(3)
            hi(19)
            hi(20)
            softplus()
            conv_tanh(2)
            taps(4)
            hi(21)
            conv_tanh(3)
            taps(5)
            squares(0)
            squares(1)
            hi(22)
            hi(23)
            squares(2)
            squares(3)
            norms()
            factors()
            hi(24)
            conv_tanh(4)
            conv_tanh(5)
            v_copy(0)
            hi(25)
            decays(0)
            hi(26)
            hi(27)
            gate_tanh(0)
            decays(1)
            hi(28)
            probs(0)
            pT_copy(0)
            ti_copy(1, 0)
            ti_copy(1, 1)
            hi(29)
            hi(30)
            ti_copy(2, 0)
            heads_hi(0)
            ti_copy(2, 1)
            hi(31)
            v_copy(1)
            ti_copy(3, 0)
            hi(32)
            ti_copy(3, 1)
            probs(1)
            pT_copy(1)
            hi(33)
            hi(34)
            ti_copy(4, 0)
            probs(2)
            ti_copy(4, 1)
            gate_tanh(1)
            pT_copy(2)
            hi(35)
            ti_copy(5, 0)
            heads_hi(1)
            hi(36)
            gate_tanh(2)
            hi(37)
            probs(3)
            ti_copy(5, 1)
            gate_tanh(3)
            heads_hi(2)
            pT_copy(3)
            wT_copy(0)
            wT_copy(1)
            vnew_copy(0)
            vnew_copy(1)
            hi(38)
            hi(39)
            vnew_copy(2)
            heads_hi(3)
            o_norm(0)
            hi(40)
            vnew_copy(3)
            hi(41)
            hi(42)
            dn_hi(0)
            o_norm(1)
            hi(43)
            dn_hi(1)
            y_norm(0)
            y_norm(1)

        @block.vector
        def _(dve):
            steps = [0]

            def link(ins):
                steps[0] += 1
                ins.then_inc(dve_step, 1)
                dve.wait_ge(dve_step, steps[0])

            dve.memset(ones[:, :], 1.0)
            dve.memset(epsc[:, 0:1], EPS)
            dve.memset(epsc[:, 1:2], DK * EPS).then_inc(dve_init, 1)
            dve.wait_ge(prow_turned, 1)
            dve.tensor_copy(pcol[:, :], bank[7][:, 0:NROWS]).then_inc(pcol_done, 1)
            dve.wait_ge(pcol_done, 1)
            dve.tensor_scalar(convh[:, :], pcol[:, R_CONV:], 0.5, None, ALU.mult)
            dve.tensor_scalar(dnwh[:, :], pcol[:, R_DNW:R_DNW + 1], 0.5, None, ALU.mult)
            dve.wait_ge(c_tanh, 1)
            link(dve.scalar_tensor_tensor(sml[:, 8:16], sml[:, 0:8], 1.0, pcol[:, R_C:R_C + 8], ALU.add, ALU.mult))
            dve.tensor_scalar(sml[:, 24:32], sml[:, 8:16], 0.5, None, ALU.mult).then_inc(sc_done, 1)
            dve.wait_ge(sc_done, 1)

            def h_lo(q):
                dve.wait_ge(hhi_done, q + 1)
                k2 = slice(2 * q, 2 * q + 2)
                dve.tensor_tensor(hlo[:, k2, :], hT[:, k2, :], hhi[:, k2, :].bitcast(F32), ALU.subtract).then_inc(hlo_done, 1)

            def lo(n):
                dve.wait_ge(hi_done, n + 1)
                dve.tensor_tensor(split_u(wlo, n), raw_u(n), split_u(whi, n).bitcast(F32), ALU.subtract).then_inc(dve_lo_done, 1)

            def x_rstd():
                dve.wait_ge(xstd_done, 1)
                dve.reciprocal(sml[:, 20:22], sml[:, 18:20]).then_inc(xrstd_done, 1)

            def mod_sums(q):
                a = acc[:, q % 2, :]
                if q >= 2:
                    dve.wait_ge(mod_ready, q - 1)
                dve.wait_ge(pool_acc_done, q + 1)
                for k in range(1, NK):
                    if k in (1, 4):
                        dve.wait_ge(ada_loaded[q % 2][k // 4], 32 * (q // 2 + 1))
                    ins = dve.scalar_tensor_tensor(a, ada[q % 2][:, k, :], sml[:, 24 + k:25 + k], acc_p[:, q % 2, :] if k == 1 else a,
                                                   ALU.mult, ALU.add)
                    if k < NK - 1:
                        link(ins)
                    else:
                        ins.then_inc(acc_done, 1)

            def modulate(q):
                k2, b = slice(2 * q, 2 * q + 2), bank[6 + q % 2]
                dve.wait_ge(mod_ready, q + 1)
                dve.tensor_tensor(mod_b[:, k2], b[:, 0:2], pcol[:, R_SHIFT + 2 * q:R_SHIFT + 2 * q + 2], ALU.add)
                link(dve.tensor_tensor(sml[:, 32:34], b[:, 2:4], pcol[:, R_SCALE + 2 * q:R_SCALE + 2 * q + 2], ALU.add))
                dve.scalar_tensor_tensor(mod_a[:, k2], sml[:, 32:34], 1.0, pcol[:, R_PRE + 2 * q:R_PRE + 2 * q + 2],
                                         ALU.add, ALU.mult).then_inc(mod_read, 1)
                dve.wait_ge(mod_read, q + 1)
                dve.wait_ge(xT_done, q + 1)
                for k in (2 * q, 2 * q + 1):
                    ins = dve.tensor_scalar(hT[:, k, :], xT[:, k, :], mod_a[:, k:k + 1], mod_b[:, k:k + 1], ALU.mult, ALU.add)
                ins.then_inc(h_done, 1)


            def conv(m):
                for i in (PAIRS[m], PAIRS[m] + 1):
                    b = bank[i // 2][:, (i % 2) * S:(i % 2 + 1) * S]
                    dve.wait_ge(tap_done, 2 * m + 2)
                    for j in range(1, 4):
                        w = convh[:, (3 - j) * NQKV + i:(3 - j) * NQKV + i + 1]
                        ins = dve.scalar_tensor_tensor(cv[:, i, j:], b[:, 0:S - j], w, cv[:, i, j:], ALU.mult, ALU.add)
                        if j < 3 or i == PAIRS[m]:
                            link(ins)
                ins.then_inc(conv_done, 1)

            def conv_silu(m):
                i = PAIRS[m]
                dve.wait_ge(ctanh_done, m + 1)
                dve.scalar_tensor_tensor(qkvs[:, i:i + 2, :], th[:, m % 2, :].rearrange("p (a s) -> p a s", a=2), 1.0, cv[:, i:i + 2, :],
                                         ALU.add, ALU.mult).then_inc(silu_done, 1)

            def gates_in():
                ba = bank[6][:, 0:16].rearrange("p (t n) -> p t n", t=NT)
                z = [zz[:, a, :].rearrange("p (t h) -> p t h", t=NT) for a in range(2)]
                dve.wait_ge(ba_ready, 1)
                dve.wait_ge(dab_loaded, 32)
                dve.tensor_scalar(z[0], ba[:, :, 0:4], -1.0, None, ALU.mult)
                link(dve.tensor_tensor(z[1], ba[:, :, 4:8], dab[:, 0:4].unsqueeze(1).to_broadcast([P, NT, DH]), ALU.add))
                dve.scalar_tensor_tensor(zz[:, 4:6, :], zz[:, 0:2, :], -1.0, zz[:, 0:2, :], ALU.mult, ALU.max).then_inc(ba_abs, 1)

            def gates_out():
                dve.wait_ge(ba_ln, 1)
                link(dve.scalar_tensor_tensor(zz[:, 2:4, :], zz[:, 0:2, :], 0.0, zz[:, 4:6, :], ALU.max, ALU.add))
                dve.tensor_scalar(cols[:, 2, :], zz[:, 2, :], -1.0, None, ALU.mult)
                dve.wait_ge(expa_done, 1)
                dve.scalar_tensor_tensor(zz[:, 0, :].rearrange("p (t h) -> p t h", t=NT), zz[:, 3, :].rearrange("p (t h) -> p t h", t=NT), -1.0,
                                         dab[:, 4:8].unsqueeze(1).to_broadcast([P, NT, DH]), ALU.mult, ALU.mult).then_inc(g_done, 1)

            def cum_copy():
                dve.wait_ge(cum_ready, 1)
                dve.tensor_copy(gcs[:, :], bank[6][:, 0:4 * NTH]).then_inc(cum_copied, 1)

            def sum_squares(j):
                dve.wait_ge(sq_done, j + 1)
                dve.tensor_reduce(ssq[:, j // 2, (j % 2) * DH:(j % 2 + 1) * DH], sq[:, j, :].rearrange("p (h n) -> p h n", h=DH), AX.X,
                                  ALU.add).then_inc(sq_summed, 1)

            def columns():
                g, gl, lk, lq, lb = gcs[:, 0:NTH], gcs[:, NTH:2 * NTH], lsq[:, 0, :], lsq[:, 1, :], cols[:, 2, :]
                dve.wait_ge(cum_copied, 1)
                dve.wait_ge(lsq_done, 2)
                dve.scalar_tensor_tensor(cols[:, 3, :], lk, 0.5, g, ALU.mult, ALU.add)
                dve.scalar_tensor_tensor(cols[:, 4, :], lq, -0.5, g, ALU.mult, ALU.add)
                dve.scalar_tensor_tensor(cols[:, 5, :], lk, -0.5, lb, ALU.mult, ALU.add)
                link(dve.scalar_tensor_tensor(cols[:, 6, :], lk, -0.5, gl, ALU.mult, ALU.add))
                dve.tensor_tensor(cols[:, 0, :], cols[:, 5, :], g, ALU.add)
                dve.tensor_tensor(cols[:, 1, :], cols[:, 6, :], g, ALU.subtract).then_inc(cols_done, 1)

            def k_tokens(t):
                dve.wait_ge(ktok_ready, t + 1)
                dve.wait_ge(ecol_done, 2)
                dve.tensor_tensor(heads(kw, t), four(2 + t), over_cols(ecol[:, 0, t * DH:(t + 1) * DH]), ALU.mult)
                dve.tensor_tensor(heads(kd, t), four(2 + t), over_cols(ecol[:, 1, t * DH:(t + 1) * DH]), ALU.mult).then_inc(ktok_used, 1)

            def v_tokens(t):
                dve.wait_ge(vtok_ready, t + 1)
                dve.tensor_tensor(heads(vb, t), four(4 + t), over_cols(ecol[:, 2, t * DH:(t + 1) * DH]), ALU.mult).then_inc(vtok_used, 1)

            def row_sum(t):
                dve.wait_ge(rows_ready, t + 1)
                dve.wait_ge(sq_summed, 4)
                for a, b, col, mask, rev in ((0, 4, 0, C_MA, True), (1, 5, 3, C_MQ, False)):
                    if a == 1:
                        dve.wait_ge(rows_exp, t + 1)
                    for h in range(DH):
                        i = t * DH + h
                        ins = dve.scalar_tensor_tensor(dec[:, a, i, :], four(b)[:, h, :], cols[:, col, i:i + 1], cst[:, mask:mask + P],
                                                       ALU.subtract, ALU.min, reverse0=rev)
                    ins.then_inc(row_sums, 1)

            def decayed(t):
                dve.wait_ge(kk_ready, t + 1)
                dve.wait_ge(dec_done, 2 * t + 2)
                dve.tensor_tensor(heads(am, t), four(2), heads(dec[:, 0, :, :], t), ALU.mult).then_inc(a_done, 1)
                dve.tensor_tensor(heads(qkd, t), four(3), heads(dec[:, 1, :, :], t), ALU.mult).then_inc(a_done, 1)
                dve.wait_ge(rows_exp, t + 1)
                dve.tensor_tensor(heads(qd, t), heads(qd, t), qkvs[:, 0:4, t * P:(t + 1) * P], ALU.mult).then_inc(qd_done, 1)

            def mask_z(l, t):
                dve.wait_ge(silu_done, 6)
                dve.wait_ge(z_ready, NT * l + t + 1)
                z = halves(2 + 2 * t, 0) if l > 0 else four(2 + 2 * t).rearrange("p h (n two) -> p h n two", two=2)[:, :, :, 1]
                ins = dve.tensor_tensor(heads(zt, t), z,
                                        cst[:, C_LV + l * HALF:C_LV + (l + 1) * HALF].unsqueeze(1).to_broadcast([P, DH, HALF]), ALU.mult)
                ins.then_inc(z_masked, 1)
                if l == 0:
                    dve.wait_ge(z_masked, t + 1)
                    dve.wait_ge(tt_init, 1)
                    dve.tensor_tensor(heads_odd(tt, t, 0), heads_odd(tt, t, 0),
                                      heads(zt, t).rearrange("p h (n b) -> p (h n) b", b=1), ALU.subtract).then_inc(t_done, 1)

            def merge(l, t):
                dve.wait_ge(x_ready, NT * (l - 1) + t + 1)
                x_t = halves(2 + 2 * t, DH * HALF).rearrange("p h (n b) -> p (h n) b", b=1 << l)
                dve.tensor_tensor(heads_odd(tt, t, l), heads_odd(tt, t, l), x_t, ALU.subtract).then_inc(t_done, 1)

            def rope(r):
                u = ROPES[r]
                dst, i = GQK[u]
                dve.wait_ge(const_loaded, 16)
                dve.wait_ge(group_ready, u + 1)
                if r >= 1:
                    dve.wait_ge(times_sin, r)
                    dve.wait_ge(rope_done, r)
                dve.stream_shuffle(rot[:, 0, :], bank[bank_of_group(u)][:, :], [p ^ 8 if p < 16 else p for p in range(32)]).then_inc(shuffled, 1)
                link(dve.tensor_tensor(rot[:, 2, :].rearrange("p (a s) -> p a s", a=2), two(bank_of_group(u)),
                                       cst[:, C_COS:C_COS + S].unsqueeze(1).to_broadcast([P, 2, S]), ALU.mult))
                dve.wait_ge(times_sin, r + 1)
                dve.tensor_tensor(dst[:, i:i + 2, :], rot[:, 1, :].rearrange("p (a s) -> p a s", a=2),
                                  rot[:, 2, :].rearrange("p (a s) -> p a s", a=2), ALU.add).then_inc(rope_done, 1)

            def gate(i):
                u = GATES[i]
                dst, j = GG[u]
                dve.wait_ge(gtanh_done, i + 1)
                dve.scalar_tensor_tensor(dst[:, j:j + 2, :], th[:, i % 2, :].rearrange("p (a s) -> p a s", a=2), 1.0, two(bank_of_group(u)),
                                         ALU.add, ALU.mult).then_inc(gate_done, 1)

            def maxima(m):
                dve.wait_ge(s_ready, m + 1)
                for e in range(2):
                    for qt in range(NT):
                        i, o, w = 2 * (2 * m + e) + qt, qt * P, (qt + 1) * P
                        s = bank[ATT[e]][:, o:o + w]
                        ins = dve.tensor_tensor_reduce(s, s, cst[:, C_CM + 2 * P - w:C_CM + 2 * P], 1.0, -3e38, ALU.add, ALU.max,
                                                       stat[:, i:i + 1])
                link(ins)
                dve.tensor_scalar(stat[:, 16 + 4 * m:20 + 4 * m], stat[:, 4 * m:4 * m + 4], -(AD ** -0.5), None, ALU.mult).then_inc(nmax_done, 1)

            def normalise(m):
                dve.wait_ge(p_done, 4 * (m + 1))
                link(dve.reciprocal(stat[:, 72 + 4 * m:76 + 4 * m], stat[:, 32 + 4 * m:36 + 4 * m]))
                for e in range(2):
                    for qt in range(NT):
                        o, w, i = qt * P, (qt + 1) * P, 72 + 4 * m + 2 * e + qt
                        ins = dve.tensor_scalar(pr[:, e, o:o + w], pr[:, e, o:o + w], stat[:, i:i + 1], None, ALU.mult)
                ins.then_inc(pn_done, 1)

            def gated_heads(m):
                dve.wait_ge(pv_ready, m + 1)
                dve.wait_ge(gate_done, 1 if m < 2 else 2)
                if m >= 2:
                    dve.wait_ge(oa_split, m - 1)
                dve.scalar_tensor_tensor(stg[:, m % 2, 0:S], bank[1][:, 0:S], 0.5, gm[:, m, :], ALU.mult, ALU.mult).then_inc(oa_done, 1)

            def heads_lo(m):
                dve.wait_ge(oa_hi, m + 1)
                dve.tensor_tensor(olo[:, m, :], stg[:, m % 2, 0:S], ohi[:, m, :].bitcast(F32), ALU.subtract).then_inc(oa_split, 1)

            def gate_sums(i, k0, k1):
                if i == 0 and k0 == 0:
                    dve.wait_ge(gbias_loaded, 16)
                a = accg[:, i * 512:(i + 1) * 512]
                for k in range(k0, k1):
                    if k % 4 == 0:
                        dve.wait_ge(ada_loaded[0][k // 4], 64 + 16 * (i + 1))
                    if k > 0:
                        dve.wait_ge(gate_acc, NK * i + k)
                    dve.scalar_tensor_tensor(a, ada0[:, k, :], sml[:, 24 + k:25 + k], a, ALU.mult, ALU.add).then_inc(gate_acc, 1)

            def gate_rows(i):
                dve.wait_ge(gate_ready, i + 1)
                dve.wait_ge(postw_loaded, 16)
                dve.tensor_tensor(accg[:, i * 512:(i + 1) * 512], bank[6][:, :], outb[:, 0, i * 512:(i + 1) * 512], ALU.mult).then_inc(gp_done, 1)

            def state_update(n):
                dve.wait_ge(state_ready, n + 1)
                if n == 2:
                    dve.wait_ge(o_ready, 1)
                if n == 0:
                    dve.tensor_copy(state[:, 0, :, :], four(3)).then_inc(state_done, 1)
                    return
                for h in range(DH):
                    ins = dve.scalar_tensor_tensor(state[:, n % 2, h, :], state[:, (n - 1) % 2, h, :], glx[:, n * DH + h:n * DH + h + 1],
                                                   four(3)[:, h, :], ALU.mult, ALU.add)
                ins.then_inc(state_done, 1)

            def o_sums(t):
                dve.wait_ge(osq_done, t + 1)
                dve.tensor_reduce(stat[:, 48 + 4 * t:52 + 4 * t], th[:, t, :].rearrange("p (h j) -> p h j", h=4), AX.X, ALU.add).then_inc(oss_done, 1)

            def o_scale(t):
                dve.wait_ge(ostd_done, t + 1)
                link(dve.reciprocal(stat[:, 64 + 4 * t:68 + 4 * t], stat[:, 56 + 4 * t:60 + 4 * t]))
                if t >= 1:
                    dve.wait_ge(oT_ready, t)
                dve.tensor_tensor(on[:, :, :], four(4 + t), over_cols(stat[:, 64 + 4 * t:68 + 4 * t]), ALU.mult).then_inc(on_done, 1)

            def o_gate(t):
                dve.wait_ge(oT_ready, t + 1)
                dve.wait_ge(oa_split, 4)
                dve.scalar_tensor_tensor(stg[:, t, :].rearrange("p (h s) -> p h s", h=4), four(4 + t), dnwh[:, :], gz[:, :, t * P:(t + 1) * P],
                                         ALU.mult, ALU.mult).then_inc(odn_done, 1)

            def dn_lo(t):
                dve.wait_ge(odn_hi, t + 1)
                dve.tensor_tensor(olo[:, 4:8, t * P:(t + 1) * P], stg[:, t, :].rearrange("p (h s) -> p h s", h=4),
                                  ohi[:, 4:8, t * P:(t + 1) * P].bitcast(F32), ALU.subtract).then_inc(odn_split, 1)

            def finish(t):
                dve.wait_ge(ysq_done, 2 * t + 2)
                dve.tensor_tensor(sml[:, 44 + t:45 + t], sml[:, 40 + 2 * t:41 + 2 * t], sml[:, 41 + 2 * t:42 + 2 * t], ALU.add).then_inc(ysum_done, 1)
                dve.wait_ge(gp_done, 2)
                dve.wait_ge(xres_loaded, 16)
                o = [outb[:, t, hf * 512:(hf + 1) * 512] for hf in range(2)]
                for hf in range(2):
                    dve.tensor_tensor(o[hf], bank[YB[t][hf]][:, :], accg[:, hf * 512:(hf + 1) * 512], ALU.mult).then_inc(ygate_done, 1)
                dve.wait_ge(ystd_done, t + 1)
                link(dve.reciprocal(sml[:, 48 + t:49 + t], sml[:, 46 + t:47 + t]))
                dve.wait_ge(ygate_done, 2 * t + 2)
                for hf in range(2):
                    dve.scalar_tensor_tensor(o[hf], o[hf], sml[:, 48 + t:49 + t], xres[:, t, hf * 512:(hf + 1) * 512],
                                             ALU.mult, ALU.add).then_inc(y_done, 1)

            x_rstd()
            mod_sums(0)
            lo(1)
            modulate(0)
            h_lo(0)
            mod_sums(1)
            lo(4)
            modulate(1)
            h_lo(1)
            mod_sums(2)
            lo(7)
            modulate(2)
            h_lo(2)
            mod_sums(3)
            lo(10)
            modulate(3)
            h_lo(3)
            lo(13)
            lo(16)
            conv(0)
            conv(1)
            conv_silu(0)
            conv(2)
            gates_in()
            lo(19)
            conv(3)
            conv_silu(1)
            rope(0)
            gates_out()
            conv_silu(2)
            sum_squares(0)
            conv_silu(3)
            cum_copy()
            rope(1)
            lo(22)
            sum_squares(1)
            sum_squares(2)
            sum_squares(3)
            conv(4)
            columns()
            conv(5)
            k_tokens(0)
            k_tokens(1)
            row_sum(0)
            conv_silu(4)
            conv_silu(5)
            decayed(0)
            gate(0)
            row_sum(1)
            lo(25)
            maxima(0)
            v_tokens(0)
            decayed(1)
            normalise(0)
            v_tokens(1)
            mask_z(0, 0)
            mask_z(0, 1)
            rope(2)
            mask_z(1, 0)
            lo(28)
            mask_z(1, 1)
            merge(1, 0)
            gated_heads(0)
            rope(3)
            merge(1, 1)
            mask_z(2, 0)
            gate_sums(0, 0, 4)
            heads_lo(0)
            lo(31)
            mask_z(2, 1)
            merge(2, 0)
            maxima(1)
            merge(2, 1)
            mask_z(3, 0)
            mask_z(3, 1)
            merge(3, 0)
            normalise(1)
            merge(3, 1)
            gate_sums(0, 4, 8)
            gated_heads(1)
            maxima(2)
            mask_z(4, 0)
            mask_z(4, 1)
            normalise(2)
            gate(1)
            merge(4, 0)
            merge(4, 1)
            gate_sums(1, 0, 4)
            gate_sums(1, 4, 8)
            heads_lo(1)
            gated_heads(2)
            lo(34)
            maxima(3)
            mask_z(5, 0)
            mask_z(5, 1)
            normalise(3)
            merge(5, 0)
            gate(2)
            merge(5, 1)
            gate_rows(0)
            gate(3)
            gate_rows(1)
            heads_lo(2)
            state_update(0)
            gated_heads(3)
            lo(37)
            state_update(1)
            o_sums(0)
            o_scale(0)
            state_update(2)
            heads_lo(3)
            lo(40)
            o_gate(0)
            dn_lo(0)
            o_sums(1)
            o_scale(1)
            lo(43)
            o_gate(1)
            dn_lo(1)
            finish(0)
            finish(1)

        @block.tensor
        def _(pe):
            def three(out, a, b, ia, ib, start, stop, skip=False):
                pe.matmul(out, a[0][ia], b[0][ib], start=start, stop=False, skip_group_check=skip)
                pe.matmul(out, a[1][ia], b[0][ib], start=False, stop=False, skip_group_check=skip)
                return pe.matmul(out, a[0][ia], b[1][ib], start=False, stop=stop, skip_group_check=skip)

            w_parts, h_parts, o_parts = (whi, wlo), (hhi, hlo), (ohi, olo)

            pe.wait_ge(prow_loaded, 16 * 5)
            pe.wait_ge(ident_loaded, 16)
            pe.transpose(bank[7][:, 0:NROWS], prow[0:NROWS, :], ident[0:NROWS, 0:NROWS]).then_inc(prow_turned, 1)
            def x_turn(b):
                pe.wait_ge(xn_done, NT)
                for k in (2 * b, 2 * b + 1):
                    for t in range(NT):
                        ins = pe.transpose(bank[b][:, (k % 2) * S + t * P:(k % 2) * S + (t + 1) * P], xn[:, t, k * P:(k + 1) * P], ident)
                ins.then_inc(xT_ready, 1)

            def mod(q):
                pe.wait_ge(acc_done, q + 1)
                if q == 1:
                    pe.wait_ge(pcol_done, 1)
                if q >= 2:
                    pe.wait_ge(mod_read, q - 1)
                for i in range(4):
                    ins = pe.matmul(bank[6 + q % 2][:, i:i + 1], acc[:, q % 2, i * P:(i + 1) * P], ones[:, 0:1], start=True, stop=True)
                ins.then_inc(mod_ready, 1)

            def qkv_unit_tile(k, i):
                n, o = 2 * k + i // 6, (i % 6) * P
                return three(bank[i // 2][:, (i % 2) * S:(i % 2 + 1) * S], w_parts, h_parts,
                             (slice(None), n % SPL, slice(o, o + P)), (slice(None), k, slice(None)),
                             start=(k == 0 and i % 2 == 0), stop=(k == NK - 1), skip=True)

            def qkv_products(n):
                k = n // 2
                pe.wait_ge(hlo_done, k // 2 + 1)
                if k == 0:
                    pe.wait_ge(xT_done, 4)
                pe.wait_ge(*low_part(n))
                for i in range(6 * (n % 2), 6 * (n % 2) + 6):
                    ins = qkv_unit_tile(k, i)
                ins.then_inc(unit_done, 1)

            def last_qkv_products():
                k = NK - 1
                pe.wait_ge(*low_part(2 * k))
                pe.wait_ge(*low_part(2 * k + 1))
                for m, i in enumerate(PAIRS):
                    qkv_unit_tile(k, i)
                    qkv_unit_tile(k, i + 1).then_inc(qkv_ready, 1)

            def ba():
                pe.wait_ge(wba_loaded, 16)
                pe.wait_ge(h_done, 4)
                pe.wait_ge(mod_read, 3)
                for t in range(NT):
                    for k in range(NK):
                        ins = pe.matmul(bank[6][:, t * 8:t * 8 + 8], hT[:, k, t * P:(t + 1) * P], wba[:, k, :], start=(k == 0), stop=(k == NK - 1))
                ins.then_inc(ba_ready, 1)

            def half(j):
                u, n = j // 2, N1 + j
                b = bank_of_group(u)
                if j % 2 == 0:
                    if u == 0:
                        pe.wait_ge(mod_read, 4)
                    elif u == 1:
                        pe.wait_ge(conv_done, 3)
                    elif u - 2 in GQK:
                        pe.wait_ge(rope_done, ROPES.index(u - 2) + 1)
                    elif u - 2 in GV:
                        pe.wait_ge(v_copied, VS.index(u - 2) + 1)
                    else:
                        pe.wait_ge(gate_done, GATES.index(u - 2) + 1)
                pe.wait_ge(hlo_done, 4)
                pe.wait_ge(*low_part(n))
                for kk in range(4):
                    k = 4 * (j % 2) + kk
                    for i in range(2):
                        out = bank[b][:, i * S:(i + 1) * S]
                        last = kk == 3 and i == 1
                        if u in GV:
                            ins = three(out, h_parts, w_parts, (slice(None), k, slice(i * P, (i + 1) * P)),
                                        (slice(None), n % SPL, slice(kk * 256, kk * 256 + 256)),
                                        start=(k == 0 and i == 0), stop=(k == NK - 1), skip=True)
                        else:
                            ins = three(out, w_parts, h_parts, (slice(None), n % SPL, slice(kk * 256 + i * P, kk * 256 + (i + 1) * P)),
                                        (slice(None), k, slice(None)), start=(k == 0 and i == 0), stop=(k == NK - 1), skip=True)
                        if last and j % 2 == 0:
                            ins.then_inc(unit_done, 1)
                        if last and j % 2 == 1:
                            ins.then_inc(group_ready, 1)

            def cum():
                g = zz[:, 0, :]
                pe.wait_ge(const_loaded, 16)
                pe.wait_ge(g_done, 1)
                pe.matmul(bank[6][:, 0:NTH], cst[:, C_TRI:C_TRI + P], g, start=True, stop=True)
                pe.matmul(bank[6][:, NTH:2 * NTH], cst[:, C_CHK:C_CHK + P], g, start=True, stop=True)
                for r in range(2):
                    o = bank[6][:, 2 * NTH:4 * NTH].rearrange("p (t r h) -> p r t h", t=NT, r=2)[:, r]
                    ins = pe.matmul(o, cst[:, C_CHK + r * CHUNK:C_CHK + r * CHUNK + 1].to_broadcast([P, P]),
                                    g.rearrange("p (t h) -> p t h", t=NT), start=True, stop=True)
                ins.then_inc(cum_ready, 1)

            def q_turn(t):
                pe.wait_ge(silu_done, 4)
                pe.wait_ge(cum_copied, 1)
                for h in range(DH):
                    ins = pe.transpose(four((6, 1)[t])[:, h, :], qkvs[:, h, t * P:(t + 1) * P], ident)
                ins.then_inc(qtok_ready, 1)

            def k_turn(t):
                pe.wait_ge(silu_done, 2)
                for h in range(DH):
                    ins = pe.transpose(four(2 + t)[:, h, :], qkvs[:, 4 + h, t * P:(t + 1) * P], ident)
                ins.then_inc(ktok_ready, 1)

            def v_turn(t):
                pe.wait_ge(silu_done, 6)
                pe.wait_ge(row_sums, 4)
                for h in range(DH):
                    ins = pe.transpose(four(4 + t)[:, h, :], qkvs[:, 8 + h, t * P:(t + 1) * P], ident)
                ins.then_inc(vtok_ready, 1)

            def rows(t):
                pe.wait_ge(cols_done, 1)
                if t == 0:
                    pe.wait_ge(conv_done, 6)
                else:
                    pe.wait_ge(row_sums, 2)
                for b, col in ((4, 3), (5, 4)):
                    for h in range(DH):
                        i = t * DH + h
                        ins = pe.matmul(four(b)[:, h, :], cols[:, col, i:i + 1].to_broadcast([P, P]), ident, start=True, stop=True)
                ins.then_inc(rows_ready, 1)

            def kk_products(t):
                pe.wait_ge(silu_done, 4)
                if t == 0:
                    pe.wait_ge(ktok_used, 2)
                else:
                    pe.wait_ge(a_done, 2)
                for b, o in ((2, 4), (3, 0)):
                    for h in range(DH):
                        ins = pe.matmul(four(b)[:, h, :], qkvs[:, 4 + h, t * P:(t + 1) * P], qkvs[:, o + h, t * P:(t + 1) * P],
                                        start=True, stop=True)
                ins.then_inc(kk_ready, 1)

            def z_products(l, t):
                if l == 0:
                    pe.wait_ge(a_done, 4)
                    if t == 1:
                        pe.wait_ge(vtok_used, 1)
                else:
                    pe.wait_ge(t_done, NT * (l - 1) + t + 1)
                for h in range(DH):
                    i = t * DH + h
                    if l == 0:
                        ins = pe.transpose(four(2 + 2 * t)[:, h, :], am[:, i, :], ident)
                    else:
                        ins = pe.matmul(halves(2 + 2 * t, 0)[:, h, :], am[:, i, :], odd(tt[:, i, :], l), start=True, stop=True)
                ins.then_inc(z_ready, 1)

            def t_turn(l, t):
                pe.wait_ge(t_done, NT * (l - 1) + t + 1)
                if l == 1 and t == 1:
                    pe.wait_ge(vtok_used, 2)
                for h in range(DH):
                    ins = pe.transpose(four(3 + 2 * t)[:, h, :], tt[:, t * DH + h, :], ident)
                ins.then_inc(turned, 1)

            def x_products(l, t):
                pe.wait_ge(z_masked, NT * l + t + 1)
                pe.wait_ge(ti_done, NT * (l - 1) + t + 1)
                for h in range(DH):
                    i = t * DH + h
                    ins = pe.matmul(halves(2 + 2 * t, DH * HALF)[:, h, :], ti[:, i, :], zt[:, i, :], start=True, stop=True)
                ins.then_inc(x_ready, 1)

            def w_products(t):
                pe.wait_ge(t_done, NT * (LEVELS - 1) + t + 1)
                for h in range(DH):
                    i = t * DH + h
                    ins = pe.matmul(four(2 + 2 * t)[:, h, :], kw[:, i, :], tt[:, i, :], start=True, stop=True)
                ins.then_inc(wT_ready, 1)

            def u_products(t):
                pe.wait_ge(vtok_used, 2)
                if t == 0:
                    pe.wait_ge(wT_copied, 1)
                else:
                    pe.wait_ge(vnew_copied, 2)
                for h in range(DH):
                    i = t * DH + h
                    ins = pe.matmul(four(2)[:, h, :], tt[:, i, :], vb[:, i, :], start=(h == 0), stop=(t == 0 and h == DH - 1),
                                    skip_group_check=True)
                if t == 0:
                    ins.then_inc(vnew_ready, 1)

            def vnew_products(n):
                t, r = n // 2, slice((n % 2) * CHUNK, (n % 2 + 1) * CHUNK)
                pe.wait_ge(wT_copied, NT)
                pe.wait_ge(state_done, n)
                pe.wait_ge(vnew_copied, n)
                for h in range(DH):
                    i = t * DH + h
                    ins = pe.matmul(four(2)[r, h, :], wT[:, i, r], state[:, (n - 1) % 2, h, :], start=False, stop=(h == DH - 1),
                                    skip_group_check=True)
                ins.then_inc(vnew_ready, 1)

            def q_products(n):
                t, r = n // 2, slice((n % 2) * CHUNK, (n % 2 + 1) * CHUNK)
                pe.wait_ge(qd_done, t + 1)
                pe.wait_ge(state_done, n)
                for h in range(DH):
                    i = t * DH + h
                    ins = pe.matmul(four(4 + t)[r, h, :], qd[:, i, r], state[:, (n - 1) % 2, h, :], start=(t == 1 and h == 0),
                                    stop=(t == 0 and h == DH - 1), skip_group_check=True)
                if t == 0:
                    ins.then_inc(o_ready, 1)

            def qk_products(t):
                pe.wait_ge(a_done, 4)
                pe.wait_ge(vnew_copied, 2 * t + 2)
                for h in range(DH):
                    i = t * DH + h
                    ins = pe.matmul(four(4 + t)[:, h, :], qkd[:, i, :], vnew[:, i, :], start=(t == 0 and h == 0), stop=(t == 1 and h == DH - 1),
                                    skip_group_check=True)
                if t == 1:
                    ins.then_inc(o_ready, 1)

            def state_products(n):
                t, r = n // 2, slice((n % 2) * CHUNK, (n % 2 + 1) * CHUNK)
                pe.wait_ge(vnew_copied, n + 1)
                for h in range(DH):
                    i = t * DH + h
                    ins = pe.matmul(four(3)[:, h, :], kd[r, i, :], vnew[r, i, :], start=True, stop=True)
                ins.then_inc(state_ready, 1)

            def o_turn(t):
                pe.wait_ge(on_done, t + 1)
                for h in range(DH):
                    ins = pe.transpose(four(4 + t)[:, h, :], on[:, h, :], ident)
                ins.then_inc(oT_ready, 1)

            def scores(m):
                if m < 2:
                    pe.wait_ge(rope_done, 2)
                else:
                    pe.wait_ge(rope_done, 4)
                if m == 0:
                    pe.wait_ge(conv_done, 4)
                    pe.wait_ge(sq_done, 4)
                else:
                    pe.wait_ge(oa_done, m)
                for qt in range(NT):
                    o, w = qt * P, (qt + 1) * P
                    for e in range(2):
                        r = slice(e * AD, (e + 1) * AD)
                        ins = pe.matmul(bank[ATT[e]][:, o:o + w], qT[r, m, o:o + P], kT[r, m, 0:w], start=True, stop=True)
                ins.then_inc(s_ready, 1)

            def p_turn(m):
                pe.wait_ge(pn_done, m + 1)
                for e in range(2):
                    for i in range(3):
                        ins = pe.transpose(bank[ATT[e]][:, i * P:(i + 1) * P], pr[:, e, i * P:(i + 1) * P], ident)
                ins.then_inc(pT_ready, 1)

            def pv(m):
                pe.wait_ge(v_copied, 1 if m < 2 else 2)
                pe.wait_ge(pT_copied, 2 * m + 2)
                for e in range(2):
                    r, cols_ = slice(e * AD, (e + 1) * AD), slice((2 * m + e) * AD, (2 * m + e + 1) * AD)
                    pe.matmul(bank[1][r, 0:S], vt[:, 0, cols_], pT[:, e, 0:S], start=True, stop=False, skip_group_check=True)
                    ins = pe.matmul(bank[1][r, P:S], vt[:, 1, cols_], pT[:, e, S:S + P], start=False, stop=True, skip_group_check=True)
                ins.then_inc(pv_ready, 1)

            def gate_sum(i):
                pe.wait_ge(gate_acc, NK * (i + 1))
                if i == 0:
                    pe.wait_ge(pT_copied, 8)
                else:
                    pe.wait_ge(gp_done, 1)
                pe.matmul(bank[6][:, :], ones[:, :], accg[:, i * 512:(i + 1) * 512], start=True, stop=True).then_inc(gate_ready, 1)

            def last_y_products(hf):
                t = NT - 1
                pe.wait_ge(odn_split, t + 1)
                for k in range(NK // 2, NK):
                    n = N1 + N2 + k
                    pe.wait_ge(*low_part(n))
                    ins = three(bank[YB[t][hf]][:, :], o_parts, w_parts, (slice(None), k, slice(t * P, (t + 1) * P)),
                                (slice(None), n % SPL, slice(hf * 512, (hf + 1) * 512)), start=False, stop=(k == NK - 1))
                ins.then_inc(y_ready, 1)

            def y_products(k, t):
                n = N1 + N2 + k
                pe.wait_ge(*low_part(n))
                if k < 4:
                    pe.wait_ge(oa_split, k + 1)
                else:
                    pe.wait_ge(odn_split, t + 1)
                if k == 0:
                    if t == 0:
                        pe.wait_ge(gate_done, 4)
                    else:
                        pe.wait_ge(oa_done, 4)
                        pe.wait_ge(gp_done, 2)
                for hf in range(2):
                    ins = three(bank[YB[t][hf]][:, :], o_parts, w_parts, (slice(None), k, slice(t * P, (t + 1) * P)),
                                (slice(None), n % SPL, slice(hf * 512, (hf + 1) * 512)), start=(k == 0), stop=(k == NK - 1))
                if k == NK - 1:
                    ins.then_inc(y_ready, 1)
                elif t == NT - 1:
                    ins.then_inc(unit_done, 1)

            x_turn(0)
            x_turn(1)
            mod(0)
            x_turn(2)
            x_turn(3)
            qkv_products(0)
            qkv_products(1)
            mod(1)
            qkv_products(2)
            qkv_products(3)
            qkv_products(4)
            qkv_products(5)
            mod(2)
            qkv_products(6)
            qkv_products(7)
            qkv_products(8)
            qkv_products(9)
            mod(3)
            qkv_products(10)
            qkv_products(11)
            qkv_products(12)
            qkv_products(13)
            last_qkv_products()
            ba()
            half(0)
            half(1)
            half(2)
            k_turn(0)
            k_turn(1)
            half(3)
            cum()
            q_turn(0)
            half(4)
            q_turn(1)
            half(5)
            half(6)
            half(7)
            rows(0)
            kk_products(0)
            scores(0)
            rows(1)
            kk_products(1)
            half(8)
            v_turn(0)
            half(9)
            v_turn(1)
            z_products(0, 0)
            z_products(0, 1)
            half(10)
            t_turn(1, 0)
            t_turn(1, 1)
            z_products(1, 0)
            p_turn(0)
            half(11)
            pv(0)
            z_products(1, 1)
            x_products(1, 0)
            x_products(1, 1)
            half(12)
            z_products(2, 0)
            t_turn(2, 0)
            z_products(2, 1)
            scores(1)
            t_turn(2, 1)
            half(13)
            x_products(2, 0)
            x_products(2, 1)
            t_turn(3, 0)
            z_products(3, 0)
            t_turn(3, 1)
            z_products(3, 1)
            x_products(3, 0)
            x_products(3, 1)
            z_products(4, 0)
            p_turn(1)
            t_turn(4, 0)
            half(14)
            pv(1)
            z_products(4, 1)
            scores(2)
            t_turn(4, 1)
            half(15)
            x_products(4, 0)
            x_products(4, 1)
            p_turn(2)
            z_products(5, 0)
            t_turn(5, 0)
            t_turn(5, 1)
            z_products(5, 1)
            half(16)
            pv(2)
            half(17)
            scores(3)
            half(18)
            x_products(5, 0)
            half(19)
            p_turn(3)
            x_products(5, 1)
            w_products(0)
            gate_sum(0)
            w_products(1)
            u_products(0)
            pv(3)
            gate_sum(1)
            state_products(0)
            y_products(0, 0)
            vnew_products(1)
            y_products(0, 1)
            state_products(1)
            qk_products(0)
            q_products(1)
            u_products(1)
            vnew_products(2)
            y_products(1, 0)
            state_products(2)
            y_products(1, 1)
            y_products(2, 0)
            y_products(2, 1)
            o_turn(0)
            vnew_products(3)
            q_products(2)
            q_products(3)
            y_products(3, 0)
            qk_products(1)
            y_products(3, 1)
            y_products(4, 0)
            y_products(5, 0)
            o_turn(1)
            y_products(6, 0)
            y_products(7, 0)
            last_y_products(0)
            last_y_products(1)

    return nc


def constants():
    f = np.float32
    c = np.zeros((P, NCONST), f)
    rope = AD // 4
    half = rope // 2
    inv = np.power(f(500000.0), -np.arange(0, rope, 2, dtype=f) / f(rope)).astype(f)
    ang = (np.arange(S, dtype=f)[None, :] * inv[:, None]).astype(f)
    c[:, C_COS:C_COS + S] = 1.0
    for p in range(P):
        d = p % AD
        if d < rope:
            c[p, C_COS:C_COS + S] = np.cos(ang[d % half])
            c[p, C_SIN:C_SIN + S] = (-1.0 if d < half else 1.0) * np.sin(ang[d % half])
    i, j = np.arange(P)[:, None], np.arange(P)[None, :]
    same = i // CHUNK == j // CHUNK
    c[:, C_ID:C_ID + P] = i == j
    c[:, C_TRI:C_TRI + P] = same & (i <= j)
    c[:, C_CHK:C_CHK + P] = same
    c[:, C_MA:C_MA + P] = np.where(same & (i > j), 1e30, -1e30)
    c[:, C_MQ:C_MQ + P] = np.where(same & (i <= j), 1e30, -1e30)
    c[:, C_CM + P:C_CM + 2 * P] = np.where(j <= i, 0.0, -1e30)
    for l in range(LEVELS):
        b = 1 << l
        q = np.arange(HALF)[None, :]
        q = q // b * 2 * b + b + q % b
        c[:, C_LV + l * HALF:C_LV + (l + 1) * HALF] = (i // (2 * b) == q // (2 * b)) & (i // b % 2 == 0)
    return c


_INS = ["x", "c", "ada_w", "ada_b", "pre_norm_w", "post_norm_w", "w_in", "conv_w", "a_log", "dt_bias", "dn_norm_w", "w_out"]


def kernel(**inputs):
    import concourse.bacc as bacc
    from concourse.bass_utils import run_bass_kernel_spmd

    nc = bacc.Bacc("TRN2", target_bir_lowering=False, num_devices=1)
    arrays, aps = {}, {}
    for name in _INS + ["consts"]:
        a = constants() if name == "consts" else np.ascontiguousarray(inputs[name])
        arrays[f"in_{name}"] = a
        aps[name] = nc.dram_tensor(f"in_{name}", a.shape, mybir.dt.from_np(a.dtype), kind="ExternalInput").ap()
    out = nc.dram_tensor("out_y", (1, S, D), F32, kind="ExternalOutput").ap()
    build(nc, aps["x"], aps["c"], aps["ada_w"], aps["ada_b"], aps["pre_norm_w"], aps["post_norm_w"], aps["w_in"], aps["conv_w"],
          aps["a_log"], aps["dt_bias"], aps["dn_norm_w"], aps["w_out"], aps["consts"], out)
    r = run_bass_kernel_spmd(nc, [arrays], core_ids=[0])
    return r.results[0]["out_y"]
```
